# Optimizing a Trainium2 kernel written in Bass

```python
import jax, jax.numpy as jnp
from jax import lax
import numpy as np

D_MODEL = 1024
BATCH = 1
SEQ = 512
DEPTH = 1
DEC_BATCH = 8
DEC_SEQ = 4
PAST_LEN = 4096
PAGE_SIZE = 128

RET_HEADS = 4
RET_DK = 128
RET_DV = 128
GLA_HEADS = 4
GLA_DK = 64
GLA_DV = 128
GLA_GATE_RANK = 16
GLA_GATE_TAU = 16.0
D_FF = 2816
CONV_WIDTH = 3
CHUNK = 64
ROPE_BASE = 10000.0
EPS = 1e-6

SPLIT_SIZES = (RET_HEADS * RET_DK, RET_HEADS * RET_DK, RET_HEADS * RET_DV, RET_HEADS * RET_DV,
               GLA_HEADS * GLA_DK, GLA_HEADS * GLA_DK, GLA_HEADS * GLA_DV, GLA_HEADS * GLA_DV,
               GLA_GATE_RANK, D_MODEL, D_MODEL)
D_IN = (2 * RET_HEADS * RET_DK + 2 * RET_HEADS * RET_DV + 2 * GLA_HEADS * GLA_DK
        + 2 * GLA_HEADS * GLA_DV + GLA_GATE_RANK + 2 * D_MODEL)

kernel_name = 'hybrid_retention_gla_convffn_step'

def rmsnorm(x, g):
    xf = x.astype(jnp.float32)
    y = xf * lax.rsqrt(jnp.mean(xf * xf, axis=-1, keepdims=True) + EPS)
    return (y * g.astype(jnp.float32)).astype(x.dtype)

def group_rmsnorm(o, g):
    B, L, H, dv = o.shape
    of = o.astype(jnp.float32)
    y = of * lax.rsqrt(jnp.mean(of * of, axis=-1, keepdims=True) + EPS)
    y = y.reshape(B, L, H * dv) * g.astype(jnp.float32)
    return y.astype(o.dtype)

def rotary(t, pos):
    half = t.shape[-1] // 2
    inv = ROPE_BASE ** (-jnp.arange(half, dtype=jnp.float32) / half)
    ang = pos[:, None] * inv[None, :]
    cos = jnp.cos(ang)[None, :, None, :]
    sin = jnp.sin(ang)[None, :, None, :]
    tf = t.astype(jnp.float32)
    t1, t2 = tf[..., :half], tf[..., half:]
    out = jnp.concatenate([t1 * cos - t2 * sin, t1 * sin + t2 * cos], axis=-1)
    return out.astype(t.dtype)

def chunked_gated_linear(q, k, v, log_a, s0):
    B, L, H, dk = q.shape
    dv = v.shape[-1]
    C = CHUNK if L % CHUNK == 0 else L
    n = L // C

    def to_chunks(t):
        return t.astype(jnp.float32).reshape(B, n, C, H, t.shape[-1]).transpose(1, 0, 3, 2, 4)

    qc, kc, vc, ac = to_chunks(q), to_chunks(k), to_chunks(v), to_chunks(log_a)
    mask = jnp.tril(jnp.ones((C, C), dtype=bool))

    def step(S, inp):
        qi, ki, vi, ai = inp
        b = jnp.cumsum(ai, axis=2)
        b_last = b[:, :, -1:, :]
        q_dec = qi * jnp.exp(b)
        k_dec = ki * jnp.exp(-b)
        scores = jnp.einsum('bhid,bhjd->bhij', q_dec, k_dec)
        scores = jnp.where(mask, scores, 0.0)
        o = (jnp.einsum('bhij,bhjv->bhiv', scores, vi)
             + jnp.einsum('bhid,bhdv->bhiv', q_dec, S))
        k_tail = ki * jnp.exp(b_last - b)
        S_new = (jnp.exp(b_last[:, :, 0, :])[..., None] * S
                 + jnp.einsum('bhjd,bhjv->bhdv', k_tail, vi))
        return S_new, o

    S, o = lax.scan(step, s0.astype(jnp.float32), (qc, kc, vc, ac))
    o = o.transpose(1, 0, 3, 2, 4).reshape(B, L, H, dv)
    return o.astype(v.dtype), S.astype(s0.dtype)

def causal_dwconv(u, prev, w, b):
    L = u.shape[1]
    ext = jnp.concatenate([prev.astype(u.dtype), u], axis=1)
    out = b + ext[:, 0:L] * w[0]
    for i in range(1, CONV_WIDTH):
        out = out + ext[:, i:i + L] * w[i]
    return out, ext[:, -(CONV_WIDTH - 1):]

def split_cols(p):
    outs, start = [], 0
    for s in SPLIT_SIZES:
        outs.append(p[..., start:start + s])
        start += s
    return outs

def layer(x, pos, s_ret, s_gla, conv_prev, ln1, w_in, w_gate_up, b_gate_up, g_ret, g_gla,
          w_ret_out, w_gla_out, w_o, ln2, w_up, conv_w, conv_b, w_down):
    B, L, _ = x.shape
    n = rmsnorm(x, ln1)
    proj = n @ w_in
    rq, rk, rv, rg, gq, gk, gv, gg, ga, m_r, m_g = split_cols(proj)

    rq = rotary(rq.reshape(B, L, RET_HEADS, RET_DK), pos)
    rk = rotary(rk.reshape(B, L, RET_HEADS, RET_DK), pos) * (RET_DK ** -0.5)
    rv = rv.reshape(B, L, RET_HEADS, RET_DV)
    log_gamma = jnp.log(1.0 - 2.0 ** (-5.0 - jnp.arange(RET_HEADS, dtype=jnp.float32)))
    log_g = jnp.broadcast_to(log_gamma[None, None, :, None], (B, L, RET_HEADS, RET_DK))
    o_r, s_ret_new = chunked_gated_linear(rq, rk, rv, log_g, s_ret)
    y_r = (group_rmsnorm(o_r, g_ret) * jax.nn.silu(rg)) @ w_ret_out

    z = (ga @ w_gate_up + b_gate_up).astype(jnp.float32)
    log_a = (jax.nn.log_sigmoid(z) / GLA_GATE_TAU).reshape(B, L, GLA_HEADS, GLA_DK)
    gq = gq.reshape(B, L, GLA_HEADS, GLA_DK) * (GLA_DK ** -0.5)
    gk = gk.reshape(B, L, GLA_HEADS, GLA_DK)
    gv = gv.reshape(B, L, GLA_HEADS, GLA_DV)
    o_g, s_gla_new = chunked_gated_linear(gq, gk, gv, log_a, s_gla)
    y_g = (group_rmsnorm(o_g, g_gla) * jax.nn.silu(gg)) @ w_gla_out

    mix = jax.nn.sigmoid(m_r) * y_r + jax.nn.sigmoid(m_g) * y_g
    h = x + mix @ w_o

    n2 = rmsnorm(h, ln2)
    up = n2 @ w_up
    u, vv = up[..., :D_FF], up[..., D_FF:]
    uc, conv_tail = causal_dwconv(u, conv_prev, conv_w, conv_b)
    h = h + (jax.nn.gelu(uc, approximate=False) * vv) @ w_down
    return h, s_ret_new, s_gla_new, conv_tail

def setup_inputs(seed: int = 0) -> dict:
    key = jax.random.key(seed)
    ks = jax.random.split(key, 24)
    f32 = jnp.float32

    def nrm(k, shape, scale):
        return jax.random.normal(k, shape, f32) * scale

    def gain(k, shape):
        return 1.0 + 0.02 * jax.random.normal(k, shape, f32)

    return {
        'x_prompt': nrm(ks[0], (BATCH, SEQ, D_MODEL), 1.0),
        'x_sample': nrm(ks[1], (DEC_BATCH, DEC_SEQ, D_MODEL), 1.0),
        'state_ret': nrm(ks[2], (DEPTH, DEC_BATCH, RET_HEADS, RET_DK, RET_DV), 0.3),
        'state_gla': nrm(ks[3], (DEPTH, DEC_BATCH, GLA_HEADS, GLA_DK, GLA_DV), 0.3),
        'cache_conv': nrm(ks[4], (DEPTH, DEC_BATCH, CONV_WIDTH - 1, D_FF), 1.0),
        'ln1': gain(ks[5], (DEPTH, D_MODEL)),
        'w_in': nrm(ks[6], (DEPTH, D_MODEL, D_IN), D_MODEL ** -0.5),
        'w_gate_up': nrm(ks[7], (DEPTH, GLA_GATE_RANK, GLA_HEADS * GLA_DK), GLA_GATE_RANK ** -0.5),
        'b_gate_up': nrm(ks[8], (DEPTH, GLA_HEADS * GLA_DK), 0.1),
        'g_ret': gain(ks[9], (DEPTH, RET_HEADS * RET_DV)),
        'g_gla': gain(ks[10], (DEPTH, GLA_HEADS * GLA_DV)),
        'w_ret_out': nrm(ks[11], (DEPTH, RET_HEADS * RET_DV, D_MODEL), (RET_HEADS * RET_DV) ** -0.5),
        'w_gla_out': nrm(ks[12], (DEPTH, GLA_HEADS * GLA_DV, D_MODEL), (GLA_HEADS * GLA_DV) ** -0.5),
        'w_o': nrm(ks[13], (DEPTH, D_MODEL, D_MODEL), D_MODEL ** -0.5),
        'ln2': gain(ks[14], (DEPTH, D_MODEL)),
        'w_up': nrm(ks[15], (DEPTH, D_MODEL, 2 * D_FF), D_MODEL ** -0.5),
        'conv_w': nrm(ks[16], (DEPTH, CONV_WIDTH, D_FF), CONV_WIDTH ** -0.5),
        'conv_b': nrm(ks[17], (DEPTH, D_FF), 0.02),
        'w_down': nrm(ks[18], (DEPTH, D_FF, D_MODEL), D_FF ** -0.5),
        'ln_f': gain(ks[19], (D_MODEL,)),
    }

def reference(x_prompt, x_sample, state_ret, state_gla, cache_conv, ln1, w_in, w_gate_up,
              b_gate_up, g_ret, g_gla, w_ret_out, w_gla_out, w_o, ln2, w_up, conv_w, conv_b,
              w_down, ln_f):
    Bp, Lp, _ = x_prompt.shape
    Ls = x_sample.shape[1]
    dt = x_prompt.dtype
    pos_p = jnp.arange(Lp, dtype=jnp.float32)
    pos_s = PAST_LEN + jnp.arange(Ls, dtype=jnp.float32)

    hp, hs = x_prompt, x_sample
    rp, rs, gp, gs, cp, cs = [], [], [], [], [], []
    for l in range(DEPTH):
        wl = (ln1[l], w_in[l], w_gate_up[l], b_gate_up[l], g_ret[l], g_gla[l], w_ret_out[l],
              w_gla_out[l], w_o[l], ln2[l], w_up[l], conv_w[l], conv_b[l], w_down[l])
        zr = jnp.zeros((Bp, RET_HEADS, RET_DK, RET_DV), dt)
        zg = jnp.zeros((Bp, GLA_HEADS, GLA_DK, GLA_DV), dt)
        zc = jnp.zeros((Bp, CONV_WIDTH - 1, D_FF), dt)
        hp, sr_p, sg_p, cv_p = layer(hp, pos_p, zr, zg, zc, *wl)
        hs, sr_s, sg_s, cv_s = layer(hs, pos_s, state_ret[l], state_gla[l], cache_conv[l], *wl)
        rp.append(sr_p); rs.append(sr_s)
        gp.append(sg_p); gs.append(sg_s)
        cp.append(cv_p); cs.append(cv_s)

    y_prompt = rmsnorm(hp, ln_f)
    y_sample = rmsnorm(hs, ln_f)
    return (y_prompt, y_sample, jnp.stack(rp), jnp.stack(rs), jnp.stack(gp), jnp.stack(gs),
            jnp.stack(cp), jnp.stack(cs))


_drawn_inputs = setup_inputs


def setup_inputs(seed=0):
    import zlib

    import numpy as np

    out = dict(_drawn_inputs(seed))
    spreads = {}
    factors = {'g_ret': 8.0, 'g_gla': 8.0, 'ln2': 2.74, 'conv_b': 5.473, 'ln_f': 2.84}
    for name, (base, spread) in spreads.items():
        noise = np.random.default_rng([zlib.crc32(name.encode()), seed]).standard_normal(out[name].shape)
        drawn = base * np.exp(spread * noise) if base else spread * noise
        out[name] = __import__('jax').numpy.asarray(drawn.astype(out[name].dtype))
    for name, factor in factors.items():
        out[name] = (out[name] * factor).astype(out[name].dtype)
    return out
```

```python
from contextlib import ExitStack

import numpy as np

import concourse.bass as bass
from concourse import mybir

F32 = mybir.dt.float32
F32R = mybir.dt.float32r
U32 = mybir.dt.uint32
ALU = mybir.AluOpType
ACT = mybir.ActivationFunctionType

P = 128
D_MODEL, SEQ, DEC_BATCH, DEC_SEQ, PAST_LEN = 1024, 512, 8, 4, 4096
HEADS, RET_DK, DV, GLA_DK, RANK = 4, 128, 128, 64, 16
D_FF, CONV_WIDTH, CHUNK, EPS = 2816, 3, 64, 1e-6
NS = DEC_BATCH * DEC_SEQ
NT = SEQ + NS
HALF = NT // 2
NJ = SEQ // P
NC = SEQ // CHUNK
KD = D_MODEL // P
KF = D_FF // P
UC = 256
EXT = 2 + SEQ + DEC_BATCH * (DEC_SEQ + 2)
CONV = EXT - 2

RQ, RK, RV, RG, GQ, GK, GV, GG, GA, MR = 0, 512, 1024, 1536, 2048, 2304, 2560, 3072, 3584, 3600
MG = MR + D_MODEL
HEAD_UNITS = [("gq", GQ), ("gk", GK), ("ga", GA), ("gv", GV), ("gv", GV + UC), ("rq", RQ), ("rq", RQ + UC),
              ("rk", RK), ("rk", RK + UC), ("rv", RV), ("rv", RV + UC), ("gg", GG), ("gg", GG + UC),
              ("rg", RG), ("rg", RG + UC)]
U_GATE = len(HEAD_UNITS)
U_WO = U_GATE + 12
U_UP = U_WO + 4
U_DOWN = U_UP + KF
U_END = U_DOWN + 12

V_LN1, V_LN2, V_LNF, V_GRET, V_GGLA, V_CW, V_CB = 0, 8, 16, 24, 28, 32, 32 + 3 * KF
NV = V_CB + KF

C1_ID, C1_ONE, C1_EPS, C1_N = 0, 128, 256, 264
C2_DS, C2_QD, C2_TL, C2_TLS, C2_BM, C2_U, C2_U4, C2_N = 0, 128, 256, 272, 276, 284, 412, 444


def constants():
    f = np.float32
    c1 = np.zeros((P, C1_N), f)
    c1[:, C1_ID:C1_ID + P] = np.eye(P)
    c1[:, C1_ONE:C1_ONE + P] = 1.0
    c1[:, C1_EPS] = EPS
    c2 = np.zeros((P, C2_N), np.float64)
    gamma = 1.0 - 2.0 ** (-5.0 - np.arange(HEADS))
    scale = RET_DK ** -0.5
    s = np.arange(NS)
    same = (s[:, None] // DEC_SEQ == s[None, :] // DEC_SEQ) & (s[:, None] <= s[None, :])
    j = np.arange(P)
    chunk = (j[:, None] // CHUNK == j[None, :] // CHUNK) & (j[:, None] <= j[None, :])
    decay = np.zeros((P, HEADS, SEQ))
    for h in range(HEADS):
        c2[:NS, C2_DS + NS * h:C2_DS + NS * (h + 1)] = same * gamma[h] ** (s[None, :] - s[:, None]) * scale
        c2[:, C2_QD + NS * h:C2_QD + NS * (h + 1)] = gamma[h] ** (s % DEC_SEQ + 1)
        for t in range(NJ):
            c2[:, C2_TL + HEADS * t + h] = gamma[h] ** (SEQ - 1 - P * t - j) * scale
        c2[:NS, C2_TLS + h] = gamma[h] ** (DEC_SEQ - 1 - s % DEC_SEQ) * scale
        gap = np.arange(SEQ)[None, :] - j[:, None]
        decay[:, h] = np.where(gap >= 0, gamma[h] ** np.maximum(gap, 0) * scale, 0.0)
    c2[:NS, C2_BM:C2_BM + DEC_BATCH] = s[:, None] // DEC_SEQ == np.arange(DEC_BATCH)[None, :]
    c2[:, C2_U:C2_U + P] = chunk / 16.0
    c2[:NS, C2_U4:C2_U4 + NS] = same / 16.0
    half = RET_DK // 2
    inv = (10000.0 ** (-(np.arange(half, dtype=f) / f(half)).astype(np.float64))).astype(f)
    pos = np.concatenate([np.arange(SEQ), PAST_LEN + s % DEC_SEQ]).astype(f)
    ang = (inv[:, None] * pos[None, :]).astype(f).astype(np.float64)
    rope = np.stack([np.concatenate([np.cos(ang), np.cos(ang)]), np.concatenate([-np.sin(ang), np.sin(ang)])], 1)
    return c1, c2.astype(f), decay.astype(f), rope.astype(f)


def gamma4(h):
    return float((1.0 - 2.0 ** (-5.0 - h)) ** DEC_SEQ)


class Steps:

    def __init__(self, eng, sem):
        self.eng, self.sem, self.n, self.off = eng, sem, 0, 0

    def did(self, ins):
        ins.then_inc(self.sem, 1)
        self.n += 1

    def wait(self):
        self.eng.wait_ge(self.sem, self.off + self.n)


def aux_uses():
    names = [("x", j) for j in range(NJ + 1)] + ["vec", "cache"]
    names += [s[0] if s[0] == "rstd1" else s for s in middle_order() if s[0] in PSUM_STEPS]
    names += ["rstd2"] + [("tail", i) for i in range(3)] + [("y", m) for m in range(KD)] + ["rstdf"]
    return {n: k for k, n in enumerate(names)}


PSUM_STEPS = ("rstd1", "v", "z", "zs", "b", "kt", "gs", "gu", "go", "gw", "gn", "rk", "rs0", "rs1", "ro", "rw", "rp", "rn")


def middle_order():
    after = {
        (2, 1): [("sc",)], (3, 0): [("z",), ("zs",), ("la",)], (3, 1): [("v", 0)],
        (4, 0): [("v", 1)], (4, 1): [("b", 0), ("v", 2), ("ex", 0)],
        (5, 0): [("v", 3)], (5, 1): [("kt", 0), ("gs", 0), ("rope", 0)],
        (6, 0): [("gu", 0), ("gs", 1), ("rope", 1)], (6, 1): [("go", 0), ("gw", 0), ("rope", 2)],
        (7, 0): [("go", 1), ("gw", 1), ("b", 1), ("rope", 3)], (7, 1): [("ex", 1), ("rope", 4)],
        (8, 0): [("kt", 1), ("gs", 2), ("rope", 5)], (8, 1): [("gu", 1), ("gs", 3), ("rope", 6)],
        (9, 0): [("go", 2), ("gw", 2), ("rope", 7)], (9, 1): [("go", 3), ("gw", 3), ("v", 4), ("gsq", 0)],
        (10, 0): [("rk", 0), ("rs0", 0), ("gn", 0), ("v", 5), ("gsq", 1)],
        (10, 1): [("rs1", 0), ("gn", 1), ("v", 6), ("gsq", 2)],
        (11, 0): [("ro", 0), ("rw", 0), ("v", 7)],
        (11, 1): [("rp", 0), ("rk", 1), ("gn", 2), ("rs0", 1), ("gsq", 3), ("y1", 0), ("y2", 0)],
        (12, 0): [("rs1", 1), ("gn", 3), ("rsq", 0), ("y1", 1), ("y2", 1)],
        (12, 1): [("ro", 1), ("rw", 1), ("rn", 0), ("rsq", 1), ("rp", 1), ("y1", 2), ("y2", 2)],
        (13, 0): [("rk", 2), ("rs0", 2), ("rs1", 2), ("rn", 1), ("y1", 3), ("y2", 3)],
        (13, 1): [("ro", 2), ("rw", 2), ("rsq", 2), ("rp", 2), ("y1", 4), ("y2", 4)],
        (14, 0): [("rk", 3), ("rs0", 3), ("rs1", 3), ("rn", 2), ("y1", 5), ("y2", 5)],
        (14, 1): [("ro", 3), ("rw", 3), ("rsq", 3), ("rp", 3), ("rn", 3), ("y1", 6), ("y2", 6), ("y1", 7), ("y2", 7)],
    }
    order = [("split", 0), ("n1",), ("sq1",), ("split", 1)]
    for u in range(U_GATE):
        if u > 0:
            order.append(("split", u + 1))
        for j in ((1,) if HEAD_UNITS[u][0] == "ga" else (0, 1)):
            order.append(("mt", u, j))
            if (u, j) == (0, 1):
                order.append(("rstd1",))
            order += after.get((u, j), [])
    return order


def build(nc, A, O):
    USE = aux_uses()
    ORDER = middle_order()
    ctx = ExitStack()
    base = (nc.sbuf_base + 31) // 32 * 32
    T = NT * 4

    def at(name, shape, off, dt=F32):
        return nc.alloc_sbuf_tensor_at(name, shape, dt, offset=base + off)

    UB = KD * UC * 4
    raw = [at(f"raw{s}", [P, KD, UC], UB * s) for s in range(2)]
    whi = [at(f"whi{s}", [P, KD, UC], UB * (2 + s), F32R) for s in range(2)]
    wlo = [at(f"wlo{s}", [P, KD, UC], UB * (4 + s), F32R) for s in range(2)]
    o = 6 * UB
    resid = at("resid", [P, KD, NT], o)
    a0 = o + KD * T
    nhi = at("nhi", [P, KD, NT], a0, F32R)
    nlo = at("nlo", [P, KD, NT], a0 + KD * T, F32R)
    y_nat = at("y_nat", [P, NJ, D_MODEL], a0)
    y_smp = at("y_smp", [NS, D_MODEL], a0 + NJ * D_MODEL * 4)
    tail_nat = at("tail_nat", [18, D_FF], a0 + (NJ + 1) * D_MODEL * 4)
    o = a0 + 2 * KD * T
    c1 = at("c1", [P, C1_N], o)
    vecs = at("vecs", [P, NV], o + C1_N * 4)
    o += (C1_N + NV) * 4
    rstd = at("rstd", [P, NT], o)
    rstd_col = at("rstd_col", [P, 8], o)
    R = o + T
    qk = at("qk", [P, 2 * HEADS, NT], R)
    gqk = at("gqk", [P, 4, NT], R + 8 * T)
    sq8 = at("sq8", [P, KD, NT], R)
    vg_o = R + 12 * T
    VB = (NJ + 1) * HEADS * DV * 4
    vg = at("vg", [P, NJ, HEADS * DV], vg_o)
    vgs = at("vgs", [NS, HEADS * DV], vg_o + NJ * 2048)
    vr_o = vg_o + VB
    vr = at("vr", [P, NJ, HEADS * DV], vr_o)
    vrs = at("vrs", [NS, HEADS * DV], vr_o + NJ * 2048)
    C = vr_o + VB
    yhi = at("yhi", [P, 2 * HEADS, NT], C, F32R)
    ylo = at("ylo", [P, 2 * HEADS, NT], C + 8 * T, F32R)
    x_nat = at("x_nat", [P, NJ, D_MODEL], C)
    x_smp = at("x_smp", [NS, D_MODEL], C + NJ * D_MODEL * 4)
    cache = at("cache", [2 * DEC_BATCH, D_FF], C + (NJ + 1) * D_MODEL * 4)
    g = C
    la = at("la", [P, NJ, 256], g); g += 4096
    las = at("las", [NS, 256], g); g += 1024
    gst = at("gst", [P, 2, NC, DV], g)
    az = at("az", [P, NJ, 256], g)
    azs = at("azs", [NS, 256], g + 4096); g += 8192
    s0g = at("s0g", [P, DEC_BATCH, DV], g); g += 4096
    ktn = at("ktn", [P, NJ, P], g); g += 2048
    kts = at("kts", [NS, P], g); g += 512
    gvm = at("gvm", [NS, DEC_BATCH, DV], g); g += 4096
    bcum, ebp, ebm, etl = (at(n, [P, NT], g + i * T) for i, n in enumerate(("bcum", "ebp", "ebm", "etl")))
    g += 4 * T
    o = C + 16 * T
    assert g + SEQ * 4 <= o
    vst = [at(f"vst{i}", [P, NT], o + i * T) for i in range(2)]
    dec = [at(f"dec{i}", [P, SEQ], (g, o)[i]) for i in range(2)]
    o += 2 * T
    s0r = [at(f"s0r{i}", [P, DEC_BATCH, DV], o + i * 4096) for i in range(2)]
    ga = at("ga", [32, NT], o)
    wg = at("wg", [32, 256], o + T)
    swp, rsn = at("swp", [P, NT], o + T + 1024), at("rsn", [P, NT], o + 2 * T + 1024)
    o += 8192
    sqt, acc = at("sqt", [P, NT], o), at("acc", [P, NT], o + T)
    vrow = at("vrow", [NV, P], o + 2 * T)
    gsc = [at(f"gsc{i}", [P, NJ, P], o + i * T) for i in range(2)]
    gss = [at(f"gss{i}", [NS, NS], o + i * T + 2048) for i in range(2)]
    rsc = at("rsc", [P, 1280], o)
    RS0 = [0, 512, 896, 1152]
    mx = [at(f"mx{i}", [P, NT], o + i * T) for i in range(2)]
    o += 5120
    cosT, sinT = at("cosT", [P, NT], o), at("sinT", [P, NT], o + T)
    gsq, grs = at("gsq", [P, NT], o), at("grs", [P, NT], o + T)
    hsq = [sqt, gsq]
    o += 2 * T
    c2 = at("c2", [P, C2_N], o)
    o = (o + C2_N * 4 + 31) // 32 * 32
    pt = at("pt", [P, KF, 18], o)
    END = o + KF * 18 * 4
    assert base + END <= nc.sbuf_usable_end, (base + END, nc.sbuf_usable_end)
    rkn = at("rkn", [P, NJ, P], vg_o)
    rks = at("rks", [NS, P], vg_o + 2048)
    rvm = at("rvm", [NS, DEC_BATCH, DV], vg_o + 2560)
    rqs = at("rqs", [P, NS], vg_o + 6656)
    rss = at("rss", [NS, NS], vg_o + 6784)
    rst = at("rst", [P, DV], vg_o + 6912)
    mhi = at("mhi", [P, KD, NT], R, F32R)
    mlo = at("mlo", [P, KD, NT], R + KD * T, F32R)
    gsig = at("gsig", [P, 4, NT], vr_o)
    assert R + 2 * KD * T <= vr_o
    ghi = at("ghi", [P, KF, NT], R, F32R)
    glo = at("glo", [P, KF, NT], R + KF * T, F32R)
    f = R + 2 * KF * T
    ext = at("ext", [P, EXT], f)
    cb = at("cb", [P, EXT], f + 2272)
    seqs = ext[:, 2 + SEQ:EXT].rearrange("p (b t) -> p b t", t=DEC_SEQ + 2)
    conv_seqs = cb[:, 2 + SEQ:EXT].rearrange("p (b t) -> p b t", t=DEC_SEQ + 2)[:, :, 0:DEC_SEQ]
    gl = [at(f"gl{i}", [P, NT], f + 4544 + i * T) for i in range(2)]
    assert f + 4544 + 2 * T <= o
    facc = at("facc", [P, NT], f)
    osq = [at("osq0", [P, NT], f + 3 * T), at("osq1", [P, NT], a0 + (NJ + 1) * D_MODEL * 4 + D_FF * 4)]
    fin = [at(f"fin{i}", [P, NT], f + (1 + i) * T) for i in range(2)]
    ysil = [at(f"ysil{i}", [P, NT], C + i * T if i < 2 else R + (8 + i - 2) * T) for i in range(4)]

    ident = c1[:, C1_ID:C1_ID + P]
    ones = c1[:, C1_ONE:C1_ONE + P]
    eps = c1[:, C1_EPS:C1_EPS + 1]

    def vec(i):
        return vecs[:, i:i + 1]

    mm = ctx.enter_context(nc.psum_tensor("mm", [P, 4, 512], F32))
    ax = ctx.enter_context(nc.psum_tensor("ax", [P, 4, 512], F32))

    def slot(j):
        return mm[:, 2 * j:2 * j + 2, 0:HALF]

    def halves(t):
        return t.rearrange("p (a b) -> p a b", a=2)

    def bank(name, b):
        return ax[:, 2 * (USE[name] % 2) + b, :]

    def bank2(name):
        k = 2 * (USE[name] % 2)
        return ax[:, k:k + 2, 0:HALF]

    def sem(name):
        return ctx.enter_context(nc.semaphore(name))

    c1_in, c2_in, vec_in, cache_in, rope_in, wg_in = map(sem, ("c1_in", "c2_in", "vec_in", "cache_in", "rope_in", "wg_in"))
    x_in = [sem(f"x_in{j}") for j in range(NJ + 1)]
    landed = [sem(f"landed{s}") for s in range(2)]
    hi_ready, lo_ready = sem("hi_ready"), sem("lo_ready")
    filled = [sem(f"filled{j}") for j in range(2)]
    drained = [sem(f"drained{j}") for j in range(2)]
    aux_filled = [sem(f"aux_filled{j}") for j in range(2)]
    aux_drained = [sem(f"aux_drained{j}") for j in range(2)]
    down_part = sem("down_part")
    act_step, dve_step, pool_step = sem("act_step"), sem("dve_step"), sem("pool_step")
    n_hi, n_lo = sem("n_hi"), sem("n_lo")
    x_kept = sem("x_kept")
    sq8_done, acc1_done = sem("sq8_done"), sem("acc1_done")
    sq_done, acc_done = sem("sq_done"), sem("acc_done")
    rstd_ready = sem("rstd_ready")
    ones_row, masks_clear = sem("ones_row"), sem("masks_clear")
    z_abs, ln_done, la_ready = sem("z_abs"), sem("ln_done"), sem("la_ready")
    b_gap, decays, qkd_ready = sem("b_gap"), sem("decays"), sem("qkd_ready")
    s0g_in, s0g_out, gst_out = map(sem, ("s0g_in", "s0g_out", "gst_out"))
    gvm_ready, rvm_ready = sem("gvm_ready"), sem("rvm_ready")
    osq_done, o_ready = sem("osq_done"), sem("o_ready")
    swapped, qk_ready = sem("swapped"), sem("qk_ready")
    dec_in = [sem(f"dec_in{i}") for i in range(2)]
    s0r_in = [sem(f"s0r_in{i}") for i in range(2)]
    s0r_out = [sem(f"s0r_out{i}") for i in range(2)]
    rst_out = sem("rst_out")
    silu_done, y_prod, y_hi, y_lo = map(sem, ("silu_done", "y_prod", "y_hi", "y_lo"))
    gate_done, m_sum, m_hi, m_lo = map(sem, ("gate_done", "m_sum", "m_hi", "m_lo"))
    ext_prev, ext_saved = sem("ext_prev"), sem("ext_saved")
    cb_first, conv_done, gelu_done, gl_scaled, g_hi, g_lo = map(
        sem, ("cb_first", "conv_done", "gelu_done", "gl_scaled", "g_hi", "g_lo"))
    fin_ready, conv_out, y_done, y_done_a, y_out, y_out_a = map(
        sem, ("fin_ready", "conv_out", "y_done", "y_done_a", "y_out", "y_out_a"))
    block = ctx.enter_context(nc.Block())

    def fills(j, u):
        return u + 1 if j == 1 or u < 2 else u

    F0 = [fills(j, U_GATE - 1) for j in range(2)]
    FW = [n + 16 for n in F0]
    FU = [n + 4 for n in FW]
    FD = [n + KF for n in FU]

    def aux_wait_filled(eng, name):
        k = USE[name]
        eng.wait_ge(aux_filled[k % 2], k // 2 + 1)

    def aux_wait_drained(eng, name):
        k = USE[name]
        eng.wait_ge(aux_drained[k % 2], k // 2 + 1)

    def aux_take(eng, name):
        k = USE[name]
        if k >= 2:
            eng.wait_ge(aux_drained[k % 2], k // 2)

    def filled_sem(name):
        return aux_filled[USE[name] % 2]

    def drained_sem(name):
        return aux_drained[USE[name] % 2]

    def gla_out(h):
        return gqk[:, h // 2 + 2 * (1 - h % 2), :]

    NORMS = [s for s in ORDER if s[0] in ("gn", "rn")]

    def normed(s):
        return gla_out(s[1]) if s[0] == "gn" else qk[:, s[1], :]

    def y_parts(n):
        h = n % HEADS
        return ysil[n % 2 + (0 if n < HEADS else 2)], (HEADS + h if n < HEADS else h), \
            ("gn", h) if n < HEADS else ("rn", h)

    def vdst(h):
        big, small = (vg, vgs) if h < HEADS else (vr, vrs)
        c = (h % HEADS) * DV
        return big[:, :, c:c + DV], small[:, c:c + DV]

    @block.sync
    def _(sp):
        sp.dma_start(c1[:, :], A["c1"]).then_inc(c1_in, 16)
        xp = A["x_prompt"][0].rearrange("(j p) d -> p j d", p=P)
        for j in range(NJ):
            sp.dma_start(x_nat[:, j, :], xp[:, j, :]).then_inc(x_in[j], 16)
        sp.dma_start(x_smp[:, :], A["x_sample"].rearrange("b t d -> (b t) d")).then_inc(x_in[NJ], 16)

        w_in = A["w_in"][0].rearrange("(k p) n -> p k n", p=P)
        w_o = A["w_o"][0].rearrange("(k p) n -> p k n", p=P)
        w_up = A["w_up"][0].rearrange("(k p) n -> p k n", p=P)
        w_down = A["w_down"][0].rearrange("(k p) n -> p k n", p=P)
        w_ret = A["w_ret_out"][0].rearrange("(k p) n -> p k n", p=P)
        w_gla = A["w_gla_out"][0].rearrange("(k p) n -> p k n", p=P)

        def load(s, free, first, second, n1=4, n2=4):
            if free is not None:
                if not isinstance(free, int):
                    free = sp.snap(free)
                sp.wait_ge(lo_ready, free)
            sp.dma_start(raw[s][:, 0:n1, :], first).then_inc(landed[s], 16)
            sp.dma_start(raw[s][:, n1:n1 + n2, :], second).then_inc(landed[s], 16)

        def cols(w, c):
            return w[:, 0:4, bass.ds(c, UC)], w[:, 4:8, bass.ds(c, UC)]

        for u, (_, c) in enumerate(HEAD_UNITS):
            load(u % 2, u - 1 if u >= 2 else None, *cols(w_in, c))
        with sp.Fori(1, 3) as it:
            for n in range(6):
                u, q, kind = U_GATE + n, n // 3, n % 3
                free = it * 6 + (u - 7)
                if kind == 0:
                    load(u % 2, free, *cols(w_in, it * 512 + (MR + UC * q - 512)))
                elif kind == 1:
                    load(u % 2, free, *cols(w_in, it * 512 + (MG + UC * q - 512)))
                else:
                    c = bass.ds(it * 512 + (UC * q - 512), UC)
                    load(u % 2, free, w_ret[:, :, c], w_gla[:, :, c])
        with sp.Fori(1, 3) as it:
            for n in range(2):
                u = U_WO + n
                load(u % 2, it * 2 + (u - 3), *cols(w_o, it * 512 + (UC * n - 512)))
        with sp.Fori(1, KF // 2 + 1) as it:
            load(U_UP % 2, it * 2 + (U_UP - 3), *cols(w_up, it * UC - UC))
            load((U_UP + 1) % 2, it * 2 + (U_UP - 2), *cols(w_up, it * UC + (D_FF - UC)))
        with sp.Fori(1, 3) as it:
            for n in range(6):
                u, q, part = U_DOWN + n, n // 3, n % 3
                c = bass.ds(it * 512 + (UC * q - 512), UC)
                k0, n2 = 8 * part, 4 if part < 2 else 2
                load(u % 2, it * 6 + (u - 7), w_down[:, k0:k0 + 4, c], w_down[:, k0 + 4:k0 + 4 + n2, c], 4, n2)

        aux_wait_drained(sp, ("tail", 2))
        sp.dma_start(O[6][0, 0], tail_nat[0:2, :]).then_inc(conv_out, 16)
        sp.dma_start(O[7][0].rearrange("b r d -> (b r) d"), tail_nat[2:18, :]).then_inc(conv_out, 16)
        yp = O[0][0].rearrange("(j p) d -> p j d", p=P)
        for n, j in enumerate((0, 2)):
            sp.wait_ge(y_done, n + 1)
            sp.dma_start(yp[:, j, :], y_nat[:, j, :]).then_inc(y_out, 16)
        sp.wait_ge(y_done, 3)
        sp.dma_start(O[1].rearrange("b t d -> (b t) d"), y_smp[:, :]).then_inc(y_out, 16)
        sp.wait_ge(conv_out, 32)
        sp.wait_ge(y_out, 48)

    @block.gpsimd
    def _(pool):
        def spread(out, v, h, ready):
            pool.tensor_tensor(out[:, :, :], v[:, h * DV:(h + 1) * DV].unsqueeze(1).to_broadcast([NS, DEC_BATCH, DV]),
                               c2[0:NS, C2_BM:C2_BM + DEC_BATCH].unsqueeze(2).to_broadcast([NS, DEC_BATCH, DV]),
                               ALU.mult).then_inc(ready, 1)

        pool.dma_start(cache[:, :], A["cache_conv"][0].rearrange("b r d -> (b r) d")).then_inc(cache_in, 16)
        pool.dma_start(c2[:, :], A["c2"]).then_inc(c2_in, 16)
        pool.dma_start(cosT[:, :], A["rope"][:, 0, :]).then_inc(rope_in, 16)
        pool.dma_start(sinT[:, :], A["rope"][:, 1, :]).then_inc(rope_in, 16)
        pool.dma_start(wg[0:RANK, :], A["w_gate_up"][0]).then_inc(wg_in, 16)
        pool.dma_start(wg[RANK:RANK + 1, :], A["b_gate_up"]).then_inc(wg_in, 16)
        pool.memset(ga[:, :], 1.0).then_inc(ones_row, 1)
        pool.wait_ge(rstd_ready, 1)
        for t in (*gsc, *gss):
            pool.memset(t[:], 0.0).then_inc(masks_clear, 1)

        for s in ORDER:
            if s[0] == "ex":
                p = s[1]
                if p == 0:
                    aux_wait_drained(pool, ("x", NJ))
                    aux_wait_drained(pool, "cache")
                else:
                    pool.wait_ge(s0g_out, 16)
                    pool.dma_start(dec[0][:, :], A["decay"][:, 0, :]).then_inc(dec_in[0], 16)
                pool.dma_start(s0g[:, :, :], A["state_gla"][0, :, 2 * p:2 * p + 2].rearrange("b r c v -> (r c) b v")
                               ).then_inc(s0g_in, 16)
                if p == 0:
                    pool.wait_ge(c2_in, 16)
                    aux_wait_drained(pool, ("v", 0))
                    spread(gvm, vgs, 0, gvm_ready)
            elif s[0] == "gu":
                aux_wait_drained(pool, s)
                p = s[1]
                pool.dma_start(O[4][0, 0, 2 * p:2 * p + 2].rearrange("r c v -> (r c) v"), gst[:, p, NC - 1, :]
                               ).then_inc(gst_out, 16)
            elif s[0] == "gw":
                h = s[1]
                if h + 1 < HEADS:
                    aux_wait_filled(pool, s)
                    aux_wait_drained(pool, ("v", h + 1))
                    spread(gvm, vgs, h + 1, gvm_ready)
                if h % 2 == 1:
                    aux_wait_drained(pool, s)
                    pool.dma_start(O[5][0, :, h - 1:h + 1].rearrange("b r c v -> (r c) b v"), s0g[:, :, :]
                                   ).then_inc(s0g_out, 16)
            elif s == ("v", 7):
                aux_wait_filled(pool, s)
                pool.dma_start(dec[1][:, :], A["decay"][:, 1, :]).then_inc(dec_in[1], 16)
            elif s == ("rk", 0):
                pool.wait_ge(qk_ready, 8)
                for h in range(2):
                    pool.dma_start(s0r[h][:, :, :], A["state_ret"][0, :, h].rearrange("b c v -> c b v")
                                   ).then_inc(s0r_in[h], 16)
                aux_wait_filled(pool, ("gw", 3))
                aux_wait_drained(pool, ("v", 4))
                spread(rvm, vrs, 0, rvm_ready)
            elif s[0] == "rw":
                h = s[1]
                if h + 1 < HEADS:
                    aux_wait_filled(pool, s)
                    aux_wait_drained(pool, ("v", HEADS + h + 1))
                    spread(rvm, vrs, h + 1, rvm_ready)
                aux_wait_drained(pool, s)
                pool.dma_start(O[3][0, :, h].rearrange("b c v -> c b v"), s0r[h % 2][:, :, :]
                               ).then_inc(s0r_out[h % 2], 16)
                if h + 2 < HEADS:
                    aux_wait_drained(pool, ("rs1", h))
                    pool.dma_start(dec[h % 2][:, :], A["decay"][:, h + 2, :]).then_inc(dec_in[h % 2], 16)
                    pool.wait_ge(s0r_out[h % 2], 16)
                    pool.dma_start(s0r[h % 2][:, :, :], A["state_ret"][0, :, h + 2].rearrange("b c v -> c b v")
                                   ).then_inc(s0r_in[h % 2], 16)
            elif s[0] == "rp":
                aux_wait_drained(pool, s)
                pool.dma_start(O[2][0, 0, s[1]], rst[:, :]).then_inc(rst_out, 16)

        with pool.Fori(0, KF // 2) as i:
            for j in range(2):
                t = i * 2 + j
                pool.wait_ge(conv_done, t + 1)
                pool.tensor_copy(seqs[:, :, 0:2].unsqueeze(1), pt[:, bass.ds(t, 1), 2:18].rearrange(
                    "p o (b t) -> p o b t", t=2)).then_inc(ext_prev, 1)
                pool.wait_ge(drained[j], i * 2 + FU[j] + 1)
                pool.wait_ge(ext_prev, t + 1)
                pool.tensor_copy(pt[:, bass.ds(t, 1), 0:2], ext[:, SEQ:SEQ + 2].unsqueeze(1)).then_inc(pool_step, 1)
                pool.tensor_copy(pt[:, bass.ds(t, 1), 2:18].rearrange("p o (b t) -> p o b t", t=2),
                                 seqs[:, :, DEC_SEQ:DEC_SEQ + 2].unsqueeze(1)).then_inc(ext_saved, 1)
            for j in range(2):
                pool.wait_ge(gelu_done, i * 2 + j + 1)
                pool.tensor_tensor(gl[j][:, :], gl[j][:, :], rstd[:, :], ALU.mult).then_inc(gl_scaled, 1)
        pool.wait_ge(gst_out, 32)
        pool.wait_ge(s0g_out, 32)
        pool.wait_ge(s0r_out[0], 32)
        pool.wait_ge(s0r_out[1], 32)
        pool.wait_ge(rst_out, 64)

    @block.scalar
    def _(act):
        st = Steps(act, act_step)

        def run(out, in_, func, done, **kw):
            return act.activation(out, in_, func, **kw).then_inc(done, 1)

        def hi(u, s, landed_count, slot_free=None):
            act.wait_ge(landed[s], landed_count)
            if slot_free is not None:
                act.wait_ge(*slot_free)
            run(whi[s][:, :, :], raw[s][:, :, :], ACT.Copy, hi_ready)

        for off, name, n in ((V_LN1, "ln1", KD), (V_LN2, "ln2", KD), (V_GRET, "g_ret", HEADS), (V_GGLA, "g_gla", HEADS),
                             (V_CB, "conv_b", KF)):
            act.dma_start(vrow[off:off + n, :], A[name][0].rearrange("(r p) -> r p", p=P)).then_inc(vec_in, 16)
        act.dma_start(vrow[V_LNF:V_LNF + KD, :], A["ln_f"].rearrange("(r p) -> r p", p=P)).then_inc(vec_in, 16)
        act.dma_start(vrow[V_CW:V_CW + 3 * KF, :], A["conv_w"][0].rearrange("i (r p) -> (i r) p", p=P)).then_inc(vec_in, 16)
        for j in range(NJ):
            aux_wait_filled(act, ("x", j))
            run(resid[:, 0:4, P * j:P * (j + 1)], bank(("x", j), 0).rearrange("p (f t) -> p f t", f=4), ACT.Copy, x_kept)
        aux_wait_filled(act, "vec")
        run(vecs[:, :], bank("vec", 0)[:, 0:NV], ACT.Copy, drained_sem("vec"))
        aux_wait_filled(act, "cache")
        run(pt[:, :, 2:18], bank("cache", 0)[:, 0:16 * KF].rearrange("p (f r) -> p f r", r=16), ACT.Copy,
            drained_sem("cache"))
        aux_wait_drained(act, ("x", NJ))
        aux_wait_drained(act, "vec")
        def square(f, places):
            n = squares[0]
            if n > 1:
                act.wait_ge(acc_done, n - 1)
            run(places[n % 2][:, :], resid[:, f, :], ACT.Square, sq_done)
            squares[0] += 1

        squares = [0]

        def root(name, width):
            aux_wait_filled(act, name)
            run(halves(rstd[:, :]), bank2(name), ACT.Sqrt, drained_sem(name), scale=1.0 / width, bias=eps)

        norms = 0
        for s in ORDER:
            k = s[0]
            if k == "split":
                u = s[1]
                hi(u, u % 2, 32 * (u // 2 + 1), (filled[1], fills(1, u - 2)) if u >= 2 else None)
            elif k == "n1":
                for f in range(KD):
                    run(nhi[:, f, :], resid[:, f, :], ACT.Copy, n_hi, scale=vec(V_LN1 + f))
            elif k == "sq1":
                run(sq8[:, :, :], resid[:, :, :], ACT.Square, sq8_done)
            elif k == "mt" and s[1] < 2:
                _, u, j = s
                act.wait_ge(filled[j], fills(j, u))
                run(halves(gqk[:, 2 * u + j, :]), slot(j), ACT.Copy, drained[j])
            elif k == "rstd1":
                root("rstd1", D_MODEL)
            elif k == "v":
                aux_wait_filled(act, s)
                big, small = vdst(s[1])
                st.did(act.activation(big, bank(s, 0).rearrange("p (j v) -> p j v", j=NJ), ACT.Copy))
                run(small, bank(s, 1)[0:NS, 0:P], ACT.Copy, drained_sem(s))
            elif k == "la":
                aux_wait_filled(act, ("z",))
                zb = 2 * (USE[("z",)] % 2)
                run(az[:, :, :].rearrange("p (b j) c -> p b (j c)", b=2), ax[:, zb:zb + 2, :], ACT.Abs, z_abs)
                aux_wait_filled(act, ("zs",))
                run(azs[:, :], bank(("zs",), 0)[0:NS, 0:256], ACT.Abs, z_abs)
                act.wait_ge(z_abs, 2)
                st.did(act.activation(az[:, :, :], az[:, :, :], ACT.Exp, scale=-1.0))
                st.did(act.activation(azs[:, :], azs[:, :], ACT.Exp, scale=-1.0))
                st.wait()
                run(az[:, :, :], az[:, :, :], ACT.Ln, ln_done, bias=1.0)
                run(azs[:, :], azs[:, :], ACT.Ln, ln_done, bias=1.0)
            elif k == "ex":
                p = s[1]
                aux_wait_filled(act, ("b", p))
                st.did(act.activation(bcum[:, 0:SEQ], bank(("b", p), 0), ACT.Copy))
                run(bcum[:, SEQ:NT], bank(("b", p), 1)[:, 0:NS], ACT.Copy, drained_sem(("b", p)))
                if p == 1:
                    aux_wait_drained(act, ("gw", 1))
                    aux_wait_filled(act, ("gs", 1))
                aux_wait_drained(act, ("b", p))
                st.did(act.activation(ebp[:, :], bcum[:, :], ACT.Exp))
                st.did(act.activation(ebm[:, :], bcum[:, :], ACT.Exp, scale=-1.0))
                act.wait_ge(b_gap, p + 1)
                run(etl[:, :], etl[:, :], ACT.Exp, decays)
            elif k == "kt":
                p = s[1]
                aux_wait_filled(act, s)
                if p == 1:
                    aux_wait_filled(act, ("gw", 1))
                st.did(act.activation(ktn[:, :, :], bank(s, 0).rearrange("p (j c) -> p j c", j=NJ), ACT.Copy))
                run(kts[:, :], bank(s, 1)[0:NS, 0:P], ACT.Copy, drained_sem(s))
            elif k == "go":
                h = s[1]
                aux_wait_filled(act, s)
                st.did(act.activation(gla_out(h)[:, 0:SEQ], bank(s, 0), ACT.Copy))
                run(gla_out(h)[:, SEQ:NT], bank(s, 1)[:, 0:NS], ACT.Copy, drained_sem(s))
            elif k in ("gsq", "rsq"):
                aux_wait_drained(act, ("go" if k == "gsq" else "ro", s[1]))
                n = NORMS.index(("gn" if k == "gsq" else "rn", s[1]))
                if n == 0:
                    act.wait_ge(qk_ready, 8)
                else:
                    aux_wait_filled(act, NORMS[n - 1])
                run(gsq[:, :], normed(NORMS[n]), ACT.Square, osq_done)
            elif k in ("gn", "rn"):
                aux_wait_filled(act, s)
                if norms > 0:
                    act.wait_ge(o_ready, norms)
                run(halves(grs[:, :]), bank2(s), ACT.Sqrt, drained_sem(s), scale=1.0 / DV, bias=eps)
                norms += 1
            elif k == "rope":
                i = s[1]
                act.wait_ge(drained[i % 2], fills(i % 2, 5 + i // 2))
                if i > 0:
                    act.wait_ge(qk_ready, i)
                half = RET_DK // 2
                st.did(act.activation(swp[0:half, :], qk[half:P, i, :], ACT.Copy))
                run(swp[half:P, :], qk[0:half, i, :], ACT.Copy, swapped)
            elif k == "ro":
                aux_wait_filled(act, s)
                st.did(act.activation(qk[:, s[1], 0:SEQ], bank(s, 0), ACT.Copy))
                run(qk[:, s[1], SEQ:NT], bank(s, 1)[:, 0:NS], ACT.Copy, drained_sem(s))
            elif k == "rp":
                aux_wait_filled(act, s)
                if s[1] > 0:
                    act.wait_ge(rst_out, 16 * s[1])
                run(rst[:, :], bank(s, 0)[:, 0:DV], ACT.Copy, drained_sem(s))
            elif k == "y1":
                n = s[1]
                u, j = 11 + n // 2, n % 2
                act.wait_ge(drained[j], fills(j, u))
                run(y_parts(n)[0][:, :], y_parts(n)[0][:, :], ACT.Silu, silu_done)
            elif k == "y2":
                n = s[1]
                if n == 0:
                    act.wait_ge(gst_out, 32)
                    act.wait_ge(s0g_out, 32)
                act.wait_ge(y_prod, n + 1)
                run(yhi[:, y_parts(n)[1], :], y_parts(n)[0][:, :], ACT.Copy, y_hi)

        with act.Fori(0, 2) as it:
            for n in range(6):
                q, kind = n // 3, n % 3
                u = U_GATE + n + 1
                done = F0[1] + 4 * q + (0, 1, 2)[kind]
                hi(u, u % 2, it * 96 + 32 * (u // 2 + 1), (filled[1], it * 8 + done))
                if kind < 2:
                    for j in range(2):
                        act.wait_ge(drained[j], it * 8 + F0[j] + 4 * q + kind + 1)
                        t = gsig[:, 2 * kind + j, :]
                        run(t, t, ACT.Sigmoid, gate_done)
                else:
                    for j in range(2):
                        act.wait_ge(m_sum, it * 4 + 2 * q + j + 1)
                        run(mhi[:, bass.ds(it * 4 + 2 * q + j, 1), :].rearrange("p o t -> p (o t)"), mx[0][:, :],
                            ACT.Copy, m_hi)
        for n in range(4):
            u = U_WO + n + 1
            hi(u, u % 2, 32 * (u // 2 + 1), (filled[1], FW[1] + n))
            for j in range(2):
                f = 2 * n + j
                act.wait_ge(drained[j], FW[j] + n + 1)
                run(nhi[:, f, :], resid[:, f, :], ACT.Copy, n_hi, scale=vec(V_LN2 + f))
                square(f, hsq)
        root("rstd2", D_MODEL)
        with act.Fori(0, KF // 2) as i:
            u = U_UP + 1
            hi(u, u % 2, i * 32 + 32 * (u // 2 + 1), (filled[1], i * 2 + FU[1]))
            for j in range(2):
                t = i * 2 + j
                act.wait_ge(drained[j], i * 2 + FU[j] + 1)
                act.wait_ge(ext_prev, t + 1)
                if j == 1:
                    act.wait_ge(gelu_done, t)
                run(cb[:, 0:CONV], ext[:, 0:CONV], ACT.Identity, cb_first, scale=vecs[:, bass.ds(t + V_CW, 1)],
                    bias=vecs[:, bass.ds(t + V_CB, 1)])
                act.wait_ge(conv_done, t + 2)
                st.did(act.activation(gl[j][:, 0:SEQ], cb[:, 0:SEQ], ACT.Gelu))
                run(gl[j][:, SEQ:NT].rearrange("p (b t) -> p b t", t=DEC_SEQ), conv_seqs, ACT.Gelu, gelu_done)
            u = U_UP + 2
            hi(u, u % 2, i * 32 + 32 * (u // 2 + 1), (filled[1], i * 2 + FU[1] + 1))
            for j in range(2):
                t = i * 2 + j
                act.wait_ge(drained[j], i * 2 + FU[j] + 2)
                run(ghi[:, bass.ds(t, 1), :].rearrange("p o t -> p (o t)"), gl[j][:, :], ACT.Copy, g_hi)
        st.n += 2 * (KF // 2 - 1)
        def y_rows(q):
            for f in (2 * q, 2 * q + 1):
                aux_wait_filled(act, ("y", f))
                st.did(act.activation(y_nat[:, :, P * f:P * (f + 1)], bank(("y", f), 0).rearrange("p (j c) -> p j c", j=NJ),
                                      ACT.Copy))
                run(y_smp[:, P * f:P * (f + 1)], bank(("y", f), 1)[0:NS, 0:P], ACT.Copy, drained_sem(("y", f)))

        for q in range(4):
            for part in range(3):
                u = U_DOWN + 3 * q + part + 1
                if u < U_END:
                    before = ((filled[1], FD[1] + q), (down_part, 2 * q + 1), (down_part, 2 * q + 2))[part]
                    hi(u, u % 2, 32 * (u // 2 + 1), before)
                if part == 0 and q == 0:
                    for i in range(3):
                        aux_wait_filled(act, ("tail", i))
                        t0, n = 8 * i, min(8, KF - 8 * i)
                        b = 2 * (USE[("tail", i)] % 2)
                        run(tail_nat[:, P * t0:P * (t0 + n)], ax[0:18, b:b + 2, :].rearrange("p a b -> p (a b)")[:, 0:P * n],
                            ACT.Copy, drained_sem(("tail", i)))
                elif part == 0:
                    y_rows(q - 1)
            for j in range(2):
                f = 2 * q + j
                act.wait_ge(drained[j], FD[j] + q + 1)
                if f >= 2:
                    aux_wait_filled(act, ("y", f - 2))
                run(fin[j][:, :], resid[:, f, :], ACT.Copy, fin_ready, scale=vec(V_LNF + f))
                square(f, osq)
        y_rows(3)
        aux_wait_filled(act, "rstdf")
        b = bank("rstdf", 0)
        st.did(act.activation(rstd_col[:, 0:NJ], b[:, 0:NJ], ACT.Sqrt, scale=1.0 / D_MODEL, bias=eps))
        run(rstd_col[0:NS, NJ:NJ + 1], b[0:NS, NJ:NJ + 1], ACT.Sqrt, drained_sem("rstdf"), scale=1.0 / D_MODEL,
            bias=eps[0:NS])
        act.wait_ge(rstd_ready, 3)
        yp = O[0][0].rearrange("(j p) d -> p j d", p=P)
        for n, j in enumerate((1, 3)):
            run(y_nat[:, j, :], y_nat[:, j, :], ACT.Copy, y_done_a, scale=rstd_col[:, j:j + 1])
            act.wait_ge(y_done_a, n + 1)
            act.dma_start(yp[:, j, :], y_nat[:, j, :]).then_inc(y_out_a, 16)
        act.wait_ge(y_out_a, 32)

    @block.vector
    def _(dve):
        st = Steps(dve, dve_step)

        def lo(u, s, count):
            dve.wait_ge(hi_ready, count)
            dve.tensor_tensor(wlo[s][:, :, :], raw[s][:, :, :], whi[s][:, :, :].bitcast(F32), ALU.subtract
                              ).then_inc(lo_ready, 1)

        def scaled(out, j, count):
            dve.wait_ge(filled[j], count)
            dve.tensor_tensor(halves(out), slot(j), halves(rstd[:, :]), ALU.mult).then_inc(drained[j], 1)

        def inverse(out, name, done):
            aux_wait_drained(dve, name)
            dve.reciprocal(out, out).then_inc(done, 1)

        adds = [0]

        def add_square(out, places, first):
            n = adds[0]
            dve.wait_ge(sq_done, n + 1)
            if first:
                dve.tensor_copy(out[:, :], places[n % 2][:, :]).then_inc(acc_done, 1)
            else:
                dve.wait_ge(acc_done, n)
                dve.tensor_tensor(out[:, :], out[:, :], places[n % 2][:, :], ALU.add).then_inc(acc_done, 1)
            adds[0] += 1

        for j in range(NJ):
            aux_wait_filled(dve, ("x", j))
            dve.wait_ge(x_kept, j + 1)
            dve.tensor_copy(resid[:, 4:8, P * j:P * (j + 1)], bank(("x", j), 1).rearrange("p (f t) -> p f t", f=4)
                            ).then_inc(drained_sem(("x", j)), 1)
        aux_wait_filled(dve, ("x", NJ))
        dve.tensor_copy(resid[:, :, SEQ:NT], bank(("x", NJ), 0)[:, 0:KD * NS].rearrange("p (f t) -> p f t", f=KD)
                        ).then_inc(drained_sem(("x", NJ)), 1)
        aux_wait_drained(dve, "vec")
        aux_wait_drained(dve, ("x", NJ))
        norms = 0
        for s in ORDER:
            k = s[0]
            if k == "split":
                lo(s[1], s[1] % 2, s[1] + 1)
            elif k == "n1":
                for f in range(KD):
                    dve.wait_ge(n_hi, f + 1)
                    dve.scalar_tensor_tensor(nlo[:, f, :], resid[:, f, :], vec(V_LN1 + f), nhi[:, f, :].bitcast(F32),
                                             op0=ALU.mult, op1=ALU.subtract).then_inc(n_lo, 1)
            elif k == "sq1":
                dve.wait_ge(sq8_done, 1)
                st.did(dve.tensor_tensor(sq8[:, 0:4, :], sq8[:, 0:4, :], sq8[:, 4:8, :], ALU.add))
                st.wait()
                st.did(dve.tensor_tensor(sq8[:, 0:2, :], sq8[:, 0:2, :], sq8[:, 2:4, :], ALU.add))
                st.wait()
                dve.tensor_tensor(acc[:, :], sq8[:, 0, :], sq8[:, 1, :], ALU.add).then_inc(acc1_done, 1)
            elif k == "rstd1":
                inverse(rstd[:, :], "rstd1", rstd_ready)
                dve.wait_ge(rstd_ready, 1)
            elif k == "sc":
                for j in range(2):
                    dve.wait_ge(drained[j], fills(j, 1))
                st.did(dve.tensor_tensor(gqk[:, :, :], gqk[:, :, :], rstd[:, :].unsqueeze(1).to_broadcast([P, 4, NT]),
                                         ALU.mult))
            elif k == "mt" and s[1] >= 2:
                _, u, j = s
                kind, n = HEAD_UNITS[u][0], fills(j, u)
                if kind == "ga":
                    dve.wait_ge(ones_row, 1)
                    dve.wait_ge(filled[1], n)
                    dve.tensor_tensor(halves(ga[0:RANK, :]), slot(1)[0:RANK], halves(rstd[0:RANK, :]), ALU.mult
                                      ).then_inc(drained[1], 1)
                elif kind in ("gv", "rv"):
                    h = 2 * (u - 3) + j if kind == "gv" else HEADS + 2 * (u - 9) + j
                    if h >= 2:
                        aux_wait_filled(dve, ("v", h - 2))
                    scaled(vst[h % 2][:, :], j, n)
                elif kind in ("gg", "rg"):
                    y = 2 * (u - 11) + j
                    if y == 0:
                        aux_wait_filled(dve, ("gw", 3))
                    if y >= 2:
                        dve.wait_ge(y_lo, y - 1)
                    scaled(y_parts(y)[0][:, :], j, n)
                else:
                    scaled(qk[:, 2 * (u - 5) + j, :], j, n)
            elif k == "la":
                dve.wait_ge(z_abs, 2)
                zb = 2 * (USE[("z",)] % 2)
                dve.tensor_scalar(la[:, :, :].rearrange("p (b j) c -> p b (j c)", b=2), ax[:, zb:zb + 2, :], 0.0, None,
                                  ALU.min).then_inc(drained_sem(("z",)), 1)
                dve.tensor_scalar(las[:, :], bank(("zs",), 0)[0:NS, 0:256], 0.0, None, ALU.min
                                  ).then_inc(drained_sem(("zs",)), 1)
                dve.wait_ge(ln_done, 2)
                aux_wait_drained(dve, ("zs",))
                aux_wait_drained(dve, ("z",))
                dve.tensor_tensor(la[:, :, :], la[:, :, :], az[:, :, :], ALU.subtract).then_inc(la_ready, 1)
                dve.tensor_tensor(las[:, :], las[:, :], azs[:, :], ALU.subtract).then_inc(la_ready, 1)
            elif k == "ex":
                p = s[1]
                aux_wait_drained(dve, ("b", p))
                if p == 1:
                    aux_wait_filled(dve, ("kt", 0))
                for a, b, c in ((0, SEQ, CHUNK), (SEQ, NT, DEC_SEQ)):
                    v = bcum[:, a:b].rearrange("p (n c) -> p n c", c=c)
                    w = etl[:, a:b].rearrange("p (n c) -> p n c", c=c)
                    ins = dve.tensor_tensor(w, v[:, :, c - 1:c].to_broadcast([P, (b - a) // c, c]), v, ALU.subtract)
                    if a == 0:
                        st.did(ins)
                    else:
                        ins.then_inc(b_gap, 1)
                dve.wait_ge(decays, p + 1)
                st.wait()
                st.did(dve.scalar_tensor_tensor(gqk[:, p, :], gqk[:, p, :], GLA_DK ** -0.5, ebp[:, :], op0=ALU.mult,
                                                op1=ALU.mult))
                st.did(dve.tensor_tensor(ebm[:, :], gqk[:, 2 + p, :], ebm[:, :], ALU.mult))
                dve.tensor_tensor(etl[:, :], gqk[:, 2 + p, :], etl[:, :], ALU.mult).then_inc(qkd_ready, 1)
            elif k == "gs":
                h = s[1]
                dve.wait_ge(masks_clear, 4)
                dve.wait_ge(c2_in, 16)
                aux_wait_filled(dve, s)
                if h >= 2:
                    aux_wait_filled(dve, ("go", h - 2))
                causal = c2[:, C2_U:C2_U + P].bitcast(U32).unsqueeze(1).to_broadcast([P, NJ, P])
                st.did(dve.copy_predicated(gsc[h % 2][:, :, :], causal, bank(s, 0).rearrange("p (j i) -> p j i", j=NJ)))
                dve.copy_predicated(gss[h % 2][:, :], c2[0:NS, C2_U4:C2_U4 + NS].bitcast(U32), bank(s, 1)[0:NS, 0:NS]
                                    ).then_inc(drained_sem(s), 1)
            elif k == "gu":
                p = s[1]
                aux_wait_filled(dve, s)
                for c in range(NC):
                    new = bank(s, c % 2)[:, (c // 2) * DV:(c // 2 + 1) * DV]
                    if c == 0:
                        st.did(dve.tensor_copy(gst[:, p, 0, :], new))
                        continue
                    st.wait()
                    last = CHUNK * (c + 1) - 1
                    ins = dve.scalar_tensor_tensor(gst[:, p, c, :], gst[:, p, c - 1, :], ebp[:, last:last + 1], new,
                                                   op0=ALU.mult, op1=ALU.add)
                    if c < NC - 1:
                        st.did(ins)
                    else:
                        ins.then_inc(drained_sem(s), 1)
            elif k == "gw":
                h = s[1]
                r = slice(GLA_DK * (h % 2), GLA_DK * (h % 2) + GLA_DK)
                aux_wait_filled(dve, s)
                end = ebp[r, SEQ + DEC_SEQ - 1:NT:DEC_SEQ].unsqueeze(2).to_broadcast([GLA_DK, DEC_BATCH, DV])
                st.did(dve.tensor_tensor(s0g[r, :, :], s0g[r, :, :], end, ALU.mult))
                st.wait()
                b = 2 * (USE[s] % 2)
                dve.tensor_tensor(s0g[r, :, :].rearrange("p (a b) v -> p a (b v)", a=2), ax[r, b:b + 2, :],
                                  s0g[r, :, :].rearrange("p (a b) v -> p a (b v)", a=2), ALU.add
                                  ).then_inc(drained_sem(s), 1)
            elif k in ("gn", "rn"):
                inverse(grs[:, :], s, dve_step)
                st.n += 1
                st.wait()
                h = s[1]
                norms += 1
                dve.scalar_tensor_tensor(normed(s), normed(s), vec((V_GGLA if k == "gn" else V_GRET) + h), grs[:, :],
                                         op0=ALU.mult, op1=ALU.mult).then_inc(o_ready, 1)
            elif k == "rope":
                i = s[1]
                if i == 0:
                    dve.wait_ge(rope_in, 32)
                dve.wait_ge(swapped, i + 1)
                dve.wait_ge(drained[i % 2], fills(i % 2, 5 + i // 2))
                st.did(dve.tensor_tensor(rsn[:, :], swp[:, :], sinT[:, :], ALU.mult))
                st.did(dve.tensor_tensor(qk[:, i, :], qk[:, i, :], cosT[:, :], ALU.mult))
                st.wait()
                dve.tensor_tensor(qk[:, i, :], qk[:, i, :], rsn[:, :], ALU.add).then_inc(qk_ready, 1)
            elif k == "rk":
                h = s[1]
                aux_wait_filled(dve, s)
                aux_wait_filled(dve, ("rp", h - 1) if h else ("gw", 3))
                tail = c2[:, C2_TL + h:C2_TL + 4 * NJ:HEADS].unsqueeze(2).to_broadcast([P, NJ, P])
                st.did(dve.tensor_tensor(rkn[:, :, :], bank(s, 0).rearrange("p (j c) -> p j c", j=NJ), tail, ALU.mult))
                dve.tensor_scalar(rks[:, :], bank(s, 1)[0:NS, 0:P], c2[0:NS, C2_TLS + h:C2_TLS + h + 1], None, ALU.mult
                                  ).then_inc(drained_sem(s), 1)
            elif k == "rs0":
                h = s[1]
                dve.wait_ge(dec_in[h % 2], 16 * (h // 2 + 1))
                aux_wait_filled(dve, s)
                aux_wait_filled(dve, ("ro", h - 1) if h else ("go", 3))
                st.did(dve.tensor_tensor(rsc[:, 0:SEQ], bank(s, 0), dec[h % 2][:, :], ALU.mult))
                dve.tensor_tensor(rsc[:, RS0[1]:RS0[2]], bank(s, 1)[:, 0:SEQ - P], dec[h % 2][:, 0:SEQ - P], ALU.mult
                                  ).then_inc(drained_sem(s), 1)
            elif k == "rs1":
                h = s[1]
                st.did(dve.tensor_tensor(rqs[:, :], qk[:, h, SEQ:NT], c2[:, C2_QD + NS * h:C2_QD + NS * (h + 1)], ALU.mult))
                aux_wait_filled(dve, s)
                st.did(dve.tensor_tensor(rsc[:, RS0[2]:RS0[3]], bank(s, 0)[:, 0:2 * P], dec[h % 2][:, 0:2 * P], ALU.mult))
                st.did(dve.tensor_tensor(rsc[:, RS0[3]:], bank(s, 0)[:, 2 * P:3 * P], dec[h % 2][:, 0:P], ALU.mult))
                dve.tensor_tensor(rss[:, :], bank(s, 1)[0:NS, 0:NS], c2[0:NS, C2_DS + NS * h:C2_DS + NS * (h + 1)],
                                  ALU.mult).then_inc(drained_sem(s), 1)
            elif k == "rw":
                h = s[1]
                aux_wait_filled(dve, s)
                b = 2 * (USE[s] % 2)
                t = s0r[h % 2][:, :, :].rearrange("p (a b) v -> p a (b v)", a=2)
                dve.scalar_tensor_tensor(t, t, gamma4(h), ax[:, b:b + 2, :], op0=ALU.mult, op1=ALU.add
                                         ).then_inc(drained_sem(s), 1)
            elif k == "y1":
                n = s[1]
                t, _, norm = y_parts(n)
                dve.wait_ge(silu_done, n + 1)
                dve.wait_ge(o_ready, NORMS.index(norm) + 1)
                dve.tensor_tensor(t[:, :], t[:, :], normed(norm), ALU.mult).then_inc(y_prod, 1)
            elif k == "y2":
                n = s[1]
                t, y, _ = y_parts(n)
                dve.wait_ge(y_hi, n + 1)
                dve.tensor_tensor(ylo[:, y, :], t[:, :], yhi[:, y, :].bitcast(F32), ALU.subtract).then_inc(y_lo, 1)

        dve.wait_ge(rst_out, 16 * HEADS)
        with dve.Fori(0, 2) as it:
            for n in range(6):
                q, kind = n // 3, n % 3
                u = U_GATE + n + 1
                lo(u, u % 2, it * 6 + (u + 1))
                if kind < 2:
                    for j in range(2):
                        if kind == 0:
                            dve.wait_ge(drained[1], it * 8 + F0[1] + 4 * q)
                        scaled(gsig[:, 2 * kind + j, :], j, it * 8 + F0[j] + 4 * q + kind + 1)
                    continue
                for j in range(2):
                    m = it * 4 + 2 * q + j
                    for b in range(2):
                        dve.wait_ge(gate_done, it * 8 + 4 * q + 3 + j)
                        dve.wait_ge(filled[b], it * 8 + F0[b] + 4 * q + 3 + j)
                        if b == 0:
                            dve.wait_ge(*((m_lo, m) if j else (lo_ready, it * 6 + (u + 1))))
                        dve.tensor_tensor(halves(mx[b][:, :]), slot(b), halves(gsig[:, 2 * b + j, :]), ALU.mult
                                          ).then_inc(drained[b], 1)
                    for b in range(2):
                        dve.wait_ge(drained[b], it * 8 + F0[b] + 4 * q + 3 + j)
                    dve.tensor_tensor(mx[0][:, :], mx[0][:, :], mx[1][:, :], ALU.add).then_inc(m_sum, 1)
                    dve.wait_ge(m_hi, m + 1)
                    dve.tensor_tensor(mlo[:, bass.ds(m, 1), :].rearrange("p o t -> p (o t)"), mx[0][:, :],
                                      mhi[:, bass.ds(m, 1), :].rearrange("p o t -> p (o t)").bitcast(F32), ALU.subtract
                                      ).then_inc(m_lo, 1)
        for n in range(4):
            u = U_WO + n + 1
            lo(u, u % 2, u + 1)
            for j in range(2):
                f = 2 * n + j
                dve.wait_ge(filled[j], FW[j] + n + 1)
                dve.tensor_tensor(halves(resid[:, f, :]), slot(j), halves(resid[:, f, :]), ALU.add).then_inc(drained[j], 1)
                dve.wait_ge(n_hi, KD + f + 1)
                dve.wait_ge(drained[j], FW[j] + n + 1)
                dve.scalar_tensor_tensor(nlo[:, f, :], resid[:, f, :], vec(V_LN2 + f), nhi[:, f, :].bitcast(F32),
                                         op0=ALU.mult, op1=ALU.subtract).then_inc(n_lo, 1)
                add_square(acc, hsq, f == 0)
        inverse(rstd[:, :], "rstd2", rstd_ready)
        dve.memset(ext[:, 0:2], 0.0).then_inc(conv_done, 1)
        dve.wait_ge(rstd_ready, 2)
        with dve.Fori(0, KF // 2) as i:
            st.off = i * 6
            u = U_UP + 1
            lo(u, u % 2, i * 2 + (u + 1))
            for j in range(2):
                t = i * 2 + j
                dve.wait_ge(conv_done, t + 1)
                dve.wait_ge(ext_prev, t + 1)
                dve.wait_ge(filled[j], i * 2 + FU[j] + 1)
                st.did(dve.tensor_tensor(ext[:, 2:2 + HALF], mm[:, 2 * j, 0:HALF], rstd[:, 0:HALF], ALU.mult))
                st.did(dve.tensor_tensor(ext[:, 2 + HALF:2 + SEQ], mm[:, 2 * j + 1, 0:SEQ - HALF], rstd[:, HALF:SEQ],
                                         ALU.mult))
                dve.tensor_tensor(seqs[:, :, 2:2 + DEC_SEQ],
                                  mm[:, 2 * j + 1, SEQ - HALF:HALF].rearrange("p (b t) -> p b t", t=DEC_SEQ),
                                  rstd[:, SEQ:NT].rearrange("p (b t) -> p b t", t=DEC_SEQ), ALU.mult
                                  ).then_inc(drained[j], 1)
                dve.wait_ge(drained[j], i * 2 + FU[j] + 1)
                dve.wait_ge(cb_first, t + 1)
                st.did(dve.scalar_tensor_tensor(cb[:, 0:CONV], ext[:, 1:1 + CONV], vecs[:, bass.ds(t + (V_CW + KF), 1)],
                                                cb[:, 0:CONV], op0=ALU.mult, op1=ALU.add))
                st.wait()
                dve.scalar_tensor_tensor(cb[:, 0:CONV], ext[:, 2:2 + CONV], vecs[:, bass.ds(t + (V_CW + 2 * KF), 1)],
                                         cb[:, 0:CONV], op0=ALU.mult, op1=ALU.add).then_inc(conv_done, 1)
            u = U_UP + 2
            lo(u, u % 2, i * 2 + (u + 1))
            for j in range(2):
                t = i * 2 + j
                dve.wait_ge(gl_scaled, t + 1)
                dve.wait_ge(filled[j], i * 2 + FU[j] + 2)
                dve.tensor_tensor(halves(gl[j][:, :]), slot(j), halves(gl[j][:, :]), ALU.mult).then_inc(drained[j], 1)
                dve.wait_ge(drained[j], i * 2 + FU[j] + 2)
                dve.wait_ge(g_hi, t + 1)
                dve.tensor_tensor(glo[:, bass.ds(t, 1), :].rearrange("p o t -> p (o t)"), gl[j][:, :],
                                  ghi[:, bass.ds(t, 1), :].rearrange("p o t -> p (o t)").bitcast(F32), ALU.subtract
                                  ).then_inc(g_lo, 1)
        st.off, st.n = 0, st.n + 6 * (KF // 2 - 1)
        for q in range(4):
            for part in range(3):
                u = U_DOWN + 3 * q + part + 1
                if u < U_END:
                    lo(u, u % 2, u + 1)
            for j in range(2):
                f = 2 * q + j
                dve.wait_ge(filled[j], FD[j] + q + 1)
                dve.tensor_tensor(halves(resid[:, f, :]), slot(j), halves(resid[:, f, :]), ALU.add).then_inc(drained[j], 1)
                add_square(facc, osq, f == 0)
        aux_wait_drained(dve, "rstdf")
        st.did(dve.reciprocal(rstd_col[:, 0:NJ], rstd_col[:, 0:NJ]))
        dve.reciprocal(rstd_col[0:NS, NJ:NJ + 1], rstd_col[0:NS, NJ:NJ + 1]).then_inc(rstd_ready, 1)
        dve.wait_ge(rstd_ready, 3)
        aux_wait_drained(dve, ("y", KD - 1))
        aux_wait_drained(dve, ("y", KD - 2))
        for j in (0, 2):
            dve.tensor_scalar(y_nat[:, j, :], y_nat[:, j, :], rstd_col[:, j:j + 1], None, ALU.mult).then_inc(y_done, 1)
        dve.tensor_scalar(y_smp[:, :], y_smp[:, :], rstd_col[0:NS, NJ:NJ + 1], None, ALU.mult).then_inc(y_done, 1)

    @block.tensor
    def _(pe):
        def product(j, s, jj, ks, xh, xl, first=True, last=True, ready=None):
            for n, (kw, kx) in enumerate(ks):
                if ready:
                    ready(kx)
                c = slice(P * jj, P * (jj + 1))
                wh, wl = whi[s][:, kw, c], wlo[s][:, kw, c]
                for m, (w, x) in enumerate(((wh, xh), (wh, xl), (wl, xh))):
                    for a in range(2):
                        ins = pe.matmul(mm[:, 2 * j + a, 0:HALF], w, x[:, kx, HALF * a:HALF * (a + 1)],
                                        start=first and n == 0 and m == 0, stop=last and n == len(ks) - 1 and m == 2)
            return ins

        every = [(k, k) for k in range(KD)]

        def small(out, w, x, start=True, stop=True, done=None):
            ins = pe.matmul(out, w, x, start=start, stop=stop, skip_group_check=True)
            if done is not None:
                ins.then_inc(done, 1)

        def turn(out, in_, done=None):
            ins = pe.transpose(out, in_, ident[0:in_.shape[0], 0:in_.shape[0]])
            if done is not None:
                ins.then_inc(done, 1)

        def turn_tokens(name, src):
            aux_take(pe, name)
            for j in range(NJ):
                turn(bank(name, 0)[:, P * j:P * (j + 1)], src[:, P * j:P * (j + 1)])
            turn(bank(name, 1)[0:NS, 0:P], src[:, SEQ:NT], filled_sem(name))

        def summed(name, sq):
            aux_take(pe, name)
            for a in range(2):
                small(bank(name, a)[:, 0:HALF], ones, sq[:, HALF * a:HALF * (a + 1)],
                      done=filled_sem(name) if a else None)

        pe.wait_ge(c1_in, 16)
        for j in range(NJ + 1):
            pe.wait_ge(x_in[j], 16)
            aux_take(pe, ("x", j))
            for f in range(KD):
                done = filled_sem(("x", j)) if f == KD - 1 else None
                if j < NJ:
                    turn(bank(("x", j), f // 4)[:, P * (f % 4):P * (f % 4 + 1)], x_nat[:, j, P * f:P * (f + 1)], done)
                else:
                    turn(bank(("x", j), 0)[:, NS * f:NS * (f + 1)], x_smp[:, P * f:P * (f + 1)], done)
        pe.wait_ge(vec_in, 112)
        aux_take(pe, "vec")
        turn(bank("vec", 0)[:, 0:NV], vrow[:, :], filled_sem("vec"))
        pe.wait_ge(cache_in, 16)
        aux_take(pe, "cache")
        for t in range(KF):
            turn(bank("cache", 0)[:, 16 * t:16 * (t + 1)], cache[:, P * t:P * (t + 1)],
                 filled_sem("cache") if t == KF - 1 else None)

        for s in ORDER:
            k = s[0]
            if k == "mt":
                _, u, j = s
                kind, n = HEAD_UNITS[u][0], fills(j, u)
                pe.wait_ge(lo_ready, u + 1)
                if n >= 2:
                    pe.wait_ge(drained[j], n - 1)
                ready = (lambda kx: pe.wait_ge(n_lo, kx + 1)) if (u, j) == (0, 0) else None
                product(j, u % 2, 0 if kind == "ga" else j, every, nhi, nlo, ready=ready).then_inc(filled[j], 1)
            elif k == "rstd1":
                pe.wait_ge(acc1_done, 1)
                summed("rstd1", acc)
            elif k == "v":
                h = s[1]
                u, j = (3 if h < HEADS else 7) + h // 2, h % 2
                pe.wait_ge(drained[j], fills(j, u))
                turn_tokens(s, vst[h % 2])
            elif k == "z":
                pe.wait_ge(wg_in, 32)
                pe.wait_ge(drained[1], fills(1, 2))
                aux_take(pe, s)
                for j in range(NJ):
                    small(bank(s, j // 2)[:, 256 * (j % 2):256 * (j % 2 + 1)], ga[0:RANK + 1, P * j:P * (j + 1)],
                          wg[0:RANK + 1, :], done=filled_sem(s) if j == NJ - 1 else None)
            elif k == "zs":
                aux_take(pe, s)
                small(bank(s, 0)[0:NS, 0:256], ga[0:RANK + 1, SEQ:NT], wg[0:RANK + 1, :], done=filled_sem(s))
            elif k == "b":
                p = s[1]
                pe.wait_ge(la_ready, 2)
                pe.wait_ge(c2_in, 16)
                aux_take(pe, s)
                for j in range(NJ):
                    small(bank(s, 0)[:, P * j:P * (j + 1)], la[:, j, P * p:P * (p + 1)], c2[:, C2_U:C2_U + P])
                small(bank(s, 1)[:, 0:NS], las[:, P * p:P * (p + 1)], c2[0:NS, C2_U4:C2_U4 + NS], done=filled_sem(s))
            elif k == "kt":
                pe.wait_ge(qkd_ready, s[1] + 1)
                turn_tokens(s, etl)
            elif k == "gs":
                h = s[1]
                r = slice(GLA_DK * (h % 2), GLA_DK * (h % 2) + GLA_DK)
                pe.wait_ge(qkd_ready, h // 2 + 1)
                aux_take(pe, s)
                for j in range(NJ):
                    c = slice(P * j, P * (j + 1))
                    small(bank(s, 0)[:, c], ebm[r, c], gqk[r, h // 2, c])
                small(bank(s, 1)[0:NS, 0:NS], ebm[r, SEQ:NT], gqk[r, h // 2, SEQ:NT], done=filled_sem(s))
            elif k == "gu":
                p = s[1]
                aux_wait_drained(pe, ("kt", p))
                aux_wait_drained(pe, ("v", 2 * p))
                aux_wait_drained(pe, ("v", 2 * p + 1))
                aux_take(pe, s)
                for h in (2 * p, 2 * p + 1):
                    o = slice(GLA_DK * (h % 2), GLA_DK * (h % 2) + GLA_DK)
                    for c in range(NC):
                        t = slice(CHUNK * (c % 2), CHUNK * (c % 2) + CHUNK)
                        small(bank(s, c % 2)[o, DV * (c // 2):DV * (c // 2 + 1)], ktn[t, c // 2, o],
                              vg[t, c // 2, DV * h:DV * (h + 1)],
                              done=filled_sem(s) if h % 2 and c == NC - 1 else None)
            elif k == "go":
                h = s[1]
                p, r = h // 2, slice(GLA_DK * (h % 2), GLA_DK * (h % 2) + GLA_DK)
                aux_wait_drained(pe, ("gs", h))
                aux_wait_drained(pe, ("gu", p))
                pe.wait_ge(s0g_in, 16 * (p + 1))
                aux_take(pe, s)
                for j in range(NJ):
                    small(bank(s, 0)[:, P * j:P * (j + 1)], vg[:, j, DV * h:DV * (h + 1)], gsc[h % 2][:, j, :], stop=False)
                    for c in (2 * j, 2 * j + 1):
                        if c > 0:
                            t = slice(CHUNK * c, CHUNK * (c + 1))
                            small(bank(s, 0)[:, t], gst[r, p, c - 1, :], gqk[r, p, t], start=False, stop=c % 2 == 1)
                small(bank(s, 1)[:, 0:NS], vgs[:, DV * h:DV * (h + 1)], gss[h % 2][:, :], stop=False)
                for b in range(DEC_BATCH):
                    t = slice(DEC_SEQ * b, DEC_SEQ * (b + 1))
                    small(bank(s, 1)[:, t], s0g[r, b, :], gqk[r, p, SEQ + DEC_SEQ * b:SEQ + DEC_SEQ * (b + 1)],
                          start=False, stop=b == DEC_BATCH - 1, done=filled_sem(s) if b == DEC_BATCH - 1 else None)
            elif k in ("gw", "rw"):
                h = s[1]
                if k == "gw":
                    o = slice(GLA_DK * (h % 2), GLA_DK * (h % 2) + GLA_DK)
                    pe.wait_ge(gvm_ready, h + 1)
                    keys, vm = kts[:, o], gvm
                else:
                    o = slice(0, P)
                    pe.wait_ge(rvm_ready, h + 1)
                    keys, vm = rks[:, :], rvm
                aux_take(pe, s)
                for a in range(2):
                    small(bank(s, a)[o, :], keys, vm[:, 4 * a:4 * (a + 1), :].rearrange("s b v -> s (b v)"),
                          done=filled_sem(s) if a else None)
            elif k in ("gn", "rn"):
                pe.wait_ge(osq_done, NORMS.index(s) + 1)
                summed(s, gsq)
            elif k == "rk":
                pe.wait_ge(qk_ready, 8)
                turn_tokens(s, qk[:, HEADS + s[1], :])
            elif k == "rs0":
                h = s[1]
                aux_take(pe, s)
                for j in range(2):
                    small(bank(s, j)[:, 0:SEQ - P * j], qk[:, HEADS + h, P * j:P * (j + 1)], qk[:, h, P * j:SEQ],
                          done=filled_sem(s) if j else None)
            elif k == "rs1":
                h = s[1]
                aux_take(pe, s)
                for j in (2, 3):
                    small(bank(s, 0)[:, 2 * P * (j - 2):2 * P * (j - 2) + SEQ - P * j],
                          qk[:, HEADS + h, P * j:P * (j + 1)], qk[:, h, P * j:SEQ])
                small(bank(s, 1)[0:NS, 0:NS], qk[:, HEADS + h, SEQ:NT], qk[:, h, SEQ:NT], done=filled_sem(s))
            elif k == "ro":
                h = s[1]
                aux_wait_drained(pe, ("rs0", h))
                aux_wait_drained(pe, ("rs1", h))
                aux_wait_drained(pe, ("v", HEADS + h))
                pe.wait_ge(s0r_in[h % 2], 16 * (h // 2 + 1))
                aux_take(pe, s)
                for j in range(NJ):
                    small(bank(s, 0)[:, P * j:SEQ], vr[:, j, DV * h:DV * (h + 1)], rsc[:, RS0[j]:RS0[j] + SEQ - P * j],
                          start=j == 0, stop=j == NJ - 1)
                small(bank(s, 1)[:, 0:NS], vrs[:, DV * h:DV * (h + 1)], rss[:, :], stop=False)
                for b in range(DEC_BATCH):
                    t = slice(DEC_SEQ * b, DEC_SEQ * (b + 1))
                    small(bank(s, 1)[:, t], s0r[h % 2][:, b, :], rqs[:, t], start=False, stop=b == DEC_BATCH - 1,
                          done=filled_sem(s) if b == DEC_BATCH - 1 else None)
            elif k == "rp":
                h = s[1]
                aux_wait_drained(pe, ("rk", h))
                aux_take(pe, s)
                for j in range(NJ):
                    small(bank(s, 0)[:, 0:DV], rkn[:, j, :], vr[:, j, DV * h:DV * (h + 1)], start=j == 0,
                          stop=j == NJ - 1, done=filled_sem(s) if j == NJ - 1 else None)

        with pe.Fori(0, 2) as it:
            for n in range(6):
                q, kind = n // 3, n % 3
                u = U_GATE + n
                pe.wait_ge(lo_ready, it * 6 + (u + 1))
                for j in range(2):
                    if kind < 2:
                        pe.wait_ge(drained[j], it * 8 + F0[j] + 4 * q + kind)
                        product(j, u % 2, j, every, nhi, nlo).then_inc(filled[j], 1)
                        continue
                    for b in range(2):
                        pe.wait_ge(drained[b], it * 8 + F0[b] + 4 * q + 2 + j)
                        if n == 2 and j == 0 and b == 0:
                            pe.wait_ge(y_lo, 2 * HEADS)
                        product(b, u % 2, j, every[4 * b:4 * b + 4], yhi, ylo).then_inc(filled[b], 1)
        with pe.Fori(0, 2) as it:
            for n in range(2):
                u = U_WO + n
                pe.wait_ge(lo_ready, it * 2 + (u + 1))
                for j in range(2):
                    pe.wait_ge(drained[j], it * 2 + (FW[j] + n))
                    ready = (lambda kx: pe.wait_ge(m_lo, kx + 1)) if n == 0 and j == 0 else None
                    product(j, u % 2, j, every, mhi, mlo, ready=ready).then_inc(filled[j], 1)

        def up(i, first=False):
            def ready(kx):
                pe.wait_ge(n_lo, KD + kx + 1)
                if kx == KD - 1:
                    pe.wait_ge(acc_done, KD)
                    summed("rstd2", acc)

            for n in range(2):
                u = U_UP + n
                pe.wait_ge(lo_ready, i * 2 + (u + 1))
                for j in range(2):
                    pe.wait_ge(drained[j], i * 2 + (FU[j] + n))
                    product(j, u % 2, j, every, nhi, nlo, ready=ready if first and n == 0 and j == 0 else None
                            ).then_inc(filled[j], 1)

        up(0, first=True)
        with pe.Fori(1, KF // 2) as i:
            up(i)

        def turn_out(q):
            for f in (2 * q, 2 * q + 1):
                pe.wait_ge(fin_ready, f + 1)
                turn_tokens(("y", f), fin[f % 2])

        for q in range(4):
            for part in range(3):
                u, k0 = U_DOWN + 3 * q + part, 8 * part
                ks = [(k, k0 + k) for k in range(min(8, KF - k0))]
                pe.wait_ge(lo_ready, u + 1)
                for j in range(2):
                    if part == 0:
                        pe.wait_ge(drained[j], FD[j] + q)
                    ready = (lambda kx: pe.wait_ge(g_lo, kx + 1)) if q == 0 and j == 0 else None
                    ins = product(j, u % 2, j, ks, ghi, glo, first=part == 0, last=part == 2, ready=ready)
                    if part == 2:
                        ins.then_inc(filled[j], 1)
                    elif j == 1:
                        ins.then_inc(down_part, 1)
                if part == 0 and q > 0:
                    turn_out(q - 1)
                if part == 0 and q == 0:
                    pe.wait_ge(ext_saved, KF)
                    for i in range(3):
                        name = ("tail", i)
                        aux_take(pe, name)
                        for t in range(8 * i, min(8 * i + 8, KF)):
                            m = t - 8 * i
                            turn(bank(name, m // 4)[0:18, P * (m % 4):P * (m % 4 + 1)], pt[:, t, :],
                                 filled_sem(name) if t == min(8 * i + 8, KF) - 1 else None)
        turn_out(3)
        pe.wait_ge(acc_done, 2 * KD)
        aux_take(pe, "rstdf")
        for j in range(NJ):
            small(bank("rstdf", 0)[:, j:j + 1], facc[:, P * j:P * (j + 1)], ones[:, 0:1])
        small(bank("rstdf", 0)[0:NS, NJ:NJ + 1], facc[:, SEQ:NT], ones[:, 0:1], done=filled_sem("rstdf"))

    ctx.close()


INPUTS = ["x_prompt", "x_sample", "state_ret", "state_gla", "cache_conv", "ln1", "w_in", "w_gate_up", "b_gate_up",
          "g_ret", "g_gla", "w_ret_out", "w_gla_out", "w_o", "ln2", "w_up", "conv_w", "conv_b", "w_down", "ln_f"]
OUTPUTS = [(1, SEQ, D_MODEL), (DEC_BATCH, DEC_SEQ, D_MODEL), (1, 1, HEADS, RET_DK, DV), (1, DEC_BATCH, HEADS, RET_DK, DV),
           (1, 1, HEADS, GLA_DK, DV), (1, DEC_BATCH, HEADS, GLA_DK, DV), (1, 1, CONV_WIDTH - 1, D_FF),
           (1, DEC_BATCH, CONV_WIDTH - 1, D_FF)]


def kernel(**inputs):
    import concourse.bacc as bacc
    from concourse.bass_utils import run_bass_kernel_spmd

    nc = bacc.Bacc("TRN2", target_bir_lowering=False, num_devices=1)
    arrays, aps = {}, {}
    for name, a in [(n, inputs[n]) for n in INPUTS] + list(zip(("c1", "c2", "decay", "rope"), constants())):
        a = np.ascontiguousarray(a)
        arrays[f"in_{name}"] = a
        aps[name] = nc.dram_tensor(f"in_{name}", a.shape, mybir.dt.from_np(a.dtype), kind="ExternalInput").ap()
    outs = [nc.dram_tensor(f"out_{i}", shape, F32, kind="ExternalOutput").ap() for i, shape in enumerate(OUTPUTS)]
    build(nc, aps, outs)
    r = run_bass_kernel_spmd(nc, [arrays], core_ids=[0])
    return tuple(r.results[0][f"out_{i}"] for i in range(len(OUTPUTS)))
```

```python
from contextlib import ExitStack

import numpy as np

import concourse.bass as bass
from concourse import mybir

F32 = mybir.dt.float32
F32R = mybir.dt.float32r
U32 = mybir.dt.uint32
ALU = mybir.AluOpType
ACT = mybir.ActivationFunctionType

P = 128
D_MODEL, SEQ, DEC_BATCH, DEC_SEQ, PAST_LEN = 1024, 512, 8, 4, 4096
HEADS, RET_DK, DV, GLA_DK, RANK = 4, 128, 128, 64, 16
D_FF, CONV_WIDTH, CHUNK, EPS = 2816, 3, 64, 1e-6
NS = DEC_BATCH * DEC_SEQ
NT = SEQ + NS
HALF = NT // 2
NJ = SEQ // P
NC = SEQ // CHUNK
KD = D_MODEL // P
KF = D_FF // P
UC = 256
EXT = 2 + SEQ + DEC_BATCH * (DEC_SEQ + 2)
CONV = EXT - 2

RQ, RK, RV, RG, GQ, GK, GV, GG, GA, MR = 0, 512, 1024, 1536, 2048, 2304, 2560, 3072, 3584, 3600
MG = MR + D_MODEL
HEAD_UNITS = [("gq", GQ), ("gk", GK), ("ga", GA), ("gv", GV), ("gv", GV + UC), ("rq", RQ), ("rq", RQ + UC),
              ("rk", RK), ("rk", RK + UC), ("rv", RV), ("rv", RV + UC), ("gg", GG), ("gg", GG + UC),
              ("rg", RG), ("rg", RG + UC)]
U_GATE = len(HEAD_UNITS)
U_WO = U_GATE + 12
U_UP = U_WO + 4
U_DOWN = U_UP + KF
U_END = U_DOWN + 12

V_LN1, V_LN2, V_LNF, V_GRET, V_GGLA, V_CW, V_CB = 0, 8, 16, 24, 28, 32, 32 + 3 * KF
NV = V_CB + KF

C1_ID, C1_ONE, C1_EPS, C1_N = 0, 128, 256, 264
C2_DS, C2_QD, C2_TL, C2_TLS, C2_BM, C2_U, C2_U4, C2_N = 0, 128, 256, 272, 276, 284, 412, 444


def constants():
    f = np.float32
    c1 = np.zeros((P, C1_N), f)
    c1[:, C1_ID:C1_ID + P] = np.eye(P)
    c1[:, C1_ONE:C1_ONE + P] = 1.0
    c1[:, C1_EPS] = EPS
    c2 = np.zeros((P, C2_N), np.float64)
    gamma = 1.0 - 2.0 ** (-5.0 - np.arange(HEADS))
    scale = RET_DK ** -0.5
    s = np.arange(NS)
    same = (s[:, None] // DEC_SEQ == s[None, :] // DEC_SEQ) & (s[:, None] <= s[None, :])
    j = np.arange(P)
    chunk = (j[:, None] // CHUNK == j[None, :] // CHUNK) & (j[:, None] <= j[None, :])
    decay = np.zeros((P, HEADS, SEQ))
    for h in range(HEADS):
        c2[:NS, C2_DS + NS * h:C2_DS + NS * (h + 1)] = same * gamma[h] ** (s[None, :] - s[:, None]) * scale
        c2[:, C2_QD + NS * h:C2_QD + NS * (h + 1)] = gamma[h] ** (s % DEC_SEQ + 1)
        for t in range(NJ):
            c2[:, C2_TL + HEADS * t + h] = gamma[h] ** (SEQ - 1 - P * t - j) * scale
        c2[:NS, C2_TLS + h] = gamma[h] ** (DEC_SEQ - 1 - s % DEC_SEQ) * scale
        gap = np.arange(SEQ)[None, :] - j[:, None]
        decay[:, h] = np.where(gap >= 0, gamma[h] ** np.maximum(gap, 0) * scale, 0.0)
    c2[:3 * NS, C2_BM:C2_BM + DEC_BATCH] = np.tile(s[:, None] // DEC_SEQ == np.arange(DEC_BATCH)[None, :], (3, 1))
    c2[:, C2_U:C2_U + P] = chunk / 16.0
    c2[:NS, C2_U4:C2_U4 + NS] = same / 16.0
    half = RET_DK // 2
    inv = (10000.0 ** (-(np.arange(half, dtype=f) / f(half)).astype(np.float64))).astype(f)
    pos = np.concatenate([np.arange(SEQ), PAST_LEN + s % DEC_SEQ]).astype(f)
    ang = (inv[:, None] * pos[None, :]).astype(f).astype(np.float64)
    rope = np.stack([np.concatenate([np.cos(ang), np.cos(ang)]), np.concatenate([-np.sin(ang), np.sin(ang)])], 1)
    return c1, c2.astype(f), decay.astype(f), rope.astype(f)


def gamma4(h):
    return float((1.0 - 2.0 ** (-5.0 - h)) ** DEC_SEQ)


class Steps:

    def __init__(self, eng, sem):
        self.eng, self.sem, self.n, self.off = eng, sem, 0, 0

    def did(self, ins):
        ins.then_inc(self.sem, 1)
        self.n += 1

    def wait(self):
        self.eng.wait_ge(self.sem, self.off + self.n)


def aux_uses():
    names = ["ln1", ("x", NJ)] + [("x", j) for j in range(NJ)]
    names += [s[0] if len(s) == 1 and s[0] in ("rstd1", "vec", "cache") else s for s in middle_order() if s[0] in PSUM_STEPS]
    names += ["rstd2"] + [("tail", i) for i in range(3)] + [("y", m) for m in range(KD - 2)] + [("ye", 0), ("ye", 1)]
    return {n: k for k, n in enumerate(names)}


PSUM_STEPS = ("rstd1", "vec", "cache", "v", "z", "zs", "b", "kt", "gs", "gu", "gx", "go", "gw", "gn", "rk", "rs0", "rs1", "ro", "rw", "rp", "rn")


def middle_order():
    after = {
        (1, 0): [("vec",)], (1, 1): [("cache",)], (2, 1): [("sc",)], (3, 0): [("z",), ("zs",), ("la",)], (3, 1): [("v", 0)],
        (4, 0): [("v", 1)], (4, 1): [("b", 0), ("v", 2), ("ex", 0)],
        (5, 0): [("v", 3)], (5, 1): [("kt", 0), ("gs", 0), ("rope", 0)],
        (6, 0): [("gu", 0), ("gs", 1), ("rope", 1)], (6, 1): [("go", 0), ("gx", 0), ("gw", 0), ("rope", 2)],
        (7, 0): [("go", 1), ("gw", 1), ("b", 1), ("rope", 3)], (7, 1): [("ex", 1), ("rope", 4)],
        (8, 0): [("kt", 1), ("gs", 2), ("rope", 5)], (8, 1): [("gu", 1), ("gs", 3), ("rope", 6)],
        (9, 0): [("go", 2), ("gx", 1), ("gw", 2), ("rope", 7)], (9, 1): [("go", 3), ("gw", 3), ("v", 4), ("gsq", 0)],
        (10, 0): [("rk", 0), ("rs0", 0), ("gn", 0), ("gsq", 1), ("v", 5), ("gi", 0)],
        (10, 1): [("rs1", 0), ("gn", 1), ("gsq", 2), ("v", 6), ("gi", 1)],
        (11, 0): [("ro", 0), ("rw", 0), ("v", 7)],
        (11, 1): [("gn", 2), ("gsq", 3), ("rp", 0), ("rk", 1), ("gi", 2)],
        (12, 0): [("gn", 3), ("rs0", 1), ("rs1", 1), ("rsq", 0), ("gi", 3)],
        (12, 1): [("ro", 1), ("rw", 1), ("rn", 0), ("rsq", 1), ("rp", 1), ("rk", 2), ("ri", 0),
                  ("sl", 0), ("sl", 1), ("sl", 2), ("y1", 0), ("y1", 1)],
        (13, 0): [("rs0", 2), ("rs1", 2), ("rn", 1), ("ri", 1), ("y1", 2), ("y2", 0), ("y2", 1)],
        (13, 1): [("ro", 2), ("rw", 2), ("rsq", 2), ("rp", 2), ("rk", 3), ("sl", 3), ("sl", 4), ("sl", 5), ("y1", 3),
                  ("y2", 2)],
        (14, 0): [("rs0", 3), ("rs1", 3), ("rn", 2), ("ri", 2), ("y2", 3), ("y1", 4), ("y1", 5), ("y2", 4)],
        (14, 1): [("ro", 3), ("rw", 3), ("rsq", 3), ("rp", 3), ("rn", 3), ("sl", 6), ("sl", 7), ("ri", 3), ("y2", 5),
                  ("y1", 6), ("y2", 6), ("y1", 7), ("y2", 7)],
    }
    order = [("n1",), ("sq1",), ("split", 1)]
    for u in range(U_GATE):
        for j in ((1,) if HEAD_UNITS[u][0] == "ga" else (0, 1)):
            order.append(("mt", u, j))
            if (u, j) == (0, 1):
                order.append(("rstd1",))
            early = u < 2 or u >= 11
            if j == 1 and early:
                order.append(("split", u + 2))
            order += after.get((u, j), [])
            if j == 1 and not early:
                order.append(("split", u + 2))
    return order


def build(nc, A, O):
    USE = aux_uses()
    ORDER = middle_order()
    ctx = ExitStack()
    base = (nc.sbuf_base + 31) // 32 * 32
    T = NT * 4

    def at(name, shape, off, dt=F32):
        return nc.alloc_sbuf_tensor_at(name, shape, dt, offset=base + off)

    UB = KD * UC * 4
    raw = [at(f"raw{s}", [P, KD, UC], UB * s) for s in range(2)]
    whi = [at(f"whi{s}", [P, KD, UC], UB * (2 + s), F32R) for s in range(2)]
    wlo = [at(f"wlo{s}", [P, KD, UC], UB * (4 + s), F32R) for s in range(2)]
    o = 6 * UB
    resid = at("resid", [P, KD, NT], o)
    a0 = o + KD * T
    nhi = at("nhi", [P, KD, NT], a0, F32R)
    nlo = at("nlo", [P, KD, NT], a0 + KD * T, F32R)
    y_nat = at("y_nat", [P, NJ, D_MODEL], a0)
    y_smp = at("y_smp", [NS, D_MODEL], a0 + NJ * D_MODEL * 4)
    tail_nat = at("tail_nat", [18, D_FF], a0 + (NJ + 1) * D_MODEL * 4)
    o = a0 + 2 * KD * T
    c1 = at("c1", [P, C1_N], o)
    vecs = at("vecs", [P, NV], o + C1_N * 4)
    o += (C1_N + NV) * 4
    rstd = at("rstd", [P, NT], o)
    rstd_col = at("rstd_col", [P, 8], o)
    R = o + T
    qk = at("qk", [P, 2 * HEADS, NT], R)
    gqk = at("gqk", [P, 4, NT], R + 8 * T)
    sq8 = at("sq8", [P, KD, NT], R)
    vg_o = R + 12 * T
    VB = (NJ + 1) * HEADS * DV * 4
    vg = at("vg", [P, NJ, HEADS * DV], vg_o)
    vgs = at("vgs", [NS, HEADS * DV], vg_o + NJ * 2048)
    vr_o = vg_o + VB
    vr = at("vr", [P, NJ, HEADS * DV], vr_o)
    vrs = at("vrs", [NS, HEADS * DV], vr_o + NJ * 2048)
    C = vr_o + VB
    yhi = at("yhi", [P, 2 * HEADS, NT], C, F32R)
    ylo = at("ylo", [P, 2 * HEADS, NT], C + 8 * T, F32R)
    x_nat = at("x_nat", [P, NJ, D_MODEL], C)
    x_smp = at("x_smp", [NS, D_MODEL], C + NJ * D_MODEL * 4)
    cache = at("cache", [2 * DEC_BATCH, D_FF], C + (NJ + 1) * D_MODEL * 4)
    g = C
    la = at("la", [P, NJ, 256], g); g += 4096
    las = at("las", [NS, 256], g); g += 1024
    gst = at("gst", [P, 2, NC, DV], g)
    az = at("az", [P, NJ, 256], g)
    azs = at("azs", [NS, 256], g + 4096); g += 8192
    s0g = at("s0g", [P, DEC_BATCH, DV], g); g += 4096
    ktn = at("ktn", [P, NJ, P], g); g += 2048
    kts = at("kts", [NS, P], g); g += 512
    gvm = at("gvm", [3 * NS, DEC_BATCH, DV], g, F32R); g += 4096
    bcum, ebp, ebm, etl = (at(n, [P, NT], g + i * T) for i, n in enumerate(("bcum", "ebp", "ebm", "etl")))
    g += 4 * T
    o = C + 16 * T
    assert g + SEQ * 4 <= o
    vst = [at(f"vst{i}", [P, NT], o + i * T) for i in range(2)]
    dec = [at(f"dec{i}", [P, SEQ], (g, o)[i]) for i in range(2)]
    o += 2 * T
    s0r = [at(f"s0r{i}", [P, DEC_BATCH, DV], o + i * 4096) for i in range(2)]
    ga = at("ga", [32, NT], o)
    wg = at("wg", [32, 256], o + T)
    swp, rsn = at("swp", [P, NT], o + T + 1024), at("rsn", [P, NT], o + 2 * T + 1024)
    o += 8192
    sqt, acc = at("sqt", [P, NT], o), at("acc", [P, NT], o + T)
    vrow = at("vrow", [NV, P], o + 2 * T)
    lnrow = at("lnrow", [KD, P], C + 16 * T)
    ln1 = at("ln1", [P, KD], C + 16 * T + 512)
    o_sc = o
    gsc = [at(f"gsc{i}", [P, NJ, P], o + i * T) for i in range(2)]
    gss = [at(f"gss{i}", [NS, NS], o + i * T + 2048) for i in range(2)]
    rsc = at("rsc", [P, 1280], o)
    RS0 = [0, 512, 896, 1152]
    mx = [at(f"mx{i}", [P, NT], o + i * T) for i in range(2)]
    o += 5120
    cosT, sinT = at("cosT", [P, NT], o), at("sinT", [P, NT], o + T)
    gsq, grs = at("gsq", [P, NT], o), at("grs", [P, NT], o + T)
    hsq = [sqt, gsq]
    o += 2 * T
    c2 = at("c2", [P, C2_N], o)
    o = (o + C2_N * 4 + 31) // 32 * 32
    pt = at("pt", [P, KF, 18], o)
    qbs = at("qbs", [P, 2, NS], o + (KF * 18 * 4 + 31) // 32 * 32 + P * 4)
    k3 = at("k3", [3 * NS, P], o + (KF * 18 * 4 + 31) // 32 * 32, F32R)
    gv3 = at("gv3", [3 * NS, DV], o_sc + 2 * T, F32R)
    END = o + (KF * 18 * 4 + 31) // 32 * 32 + P * 4 + 2 * NS * 4
    assert base + END <= nc.sbuf_usable_end, (base + END, nc.sbuf_usable_end)
    rkn = at("rkn", [P, NJ, P], vg_o)
    rks = at("rks", [NS, P], vg_o + 2048)
    rvm = at("rvm", [3 * NS, DEC_BATCH, DV], vg_o + 2560, F32R)
    rv3 = at("rv3", [3 * NS, DV], vg_o + 7424, F32R)
    assert 7424 + DV * 4 <= VB
    rqs = at("rqs", [P, NS], vg_o + 6656)
    rss = at("rss", [NS, NS], vg_o + 6784)
    rst = at("rst", [P, DV], vg_o + 6912)
    mhi = at("mhi", [P, KD, NT], R, F32R)
    mlo = at("mlo", [P, KD, NT], R + KD * T, F32R)
    gsig = at("gsig", [P, 4, NT], vr_o)
    assert R + 2 * KD * T <= vr_o
    ghi = at("ghi", [P, KF, NT], R, F32R)
    glo = at("glo", [P, KF, NT], R + KF * T, F32R)
    f = R + 2 * KF * T
    ext = at("ext", [P, EXT], f)
    cb = at("cb", [P, EXT], f + 2272)
    seqs = ext[:, 2 + SEQ:EXT].rearrange("p (b t) -> p b t", t=DEC_SEQ + 2)
    conv_seqs = cb[:, 2 + SEQ:EXT].rearrange("p (b t) -> p b t", t=DEC_SEQ + 2)[:, :, 0:DEC_SEQ]
    gl = [at(f"gl{i}", [P, NT], f + 4544 + i * T) for i in range(2)]
    assert f + 4544 + 2 * T <= o
    facc = at("facc", [P, NT], f)
    osq = [at("osq0", [P, NT], f + 3 * T), at("osq1", [P, NT], a0 + (NJ + 1) * D_MODEL * 4 + D_FF * 4)]
    fin = [at(f"fin{i}", [P, NT], f + (1 + i) * T) for i in range(2)]
    ysil = [at(f"ysil{i}", [P, NT], C + i * T if i < HEADS else R + (8 + (2, 0, 3, 1)[i - HEADS]) * T)
            for i in range(2 * HEADS)]

    ident = c1[:, C1_ID:C1_ID + P]
    ones = c1[:, C1_ONE:C1_ONE + P]
    eps = c1[:, C1_EPS:C1_EPS + 1]

    def vec(i):
        return vecs[:, i:i + 1]

    mm = ctx.enter_context(nc.psum_tensor("mm", [P, 4, 512], F32))
    ax = ctx.enter_context(nc.psum_tensor("ax", [P, 4, 512], F32))

    def slot(j):
        return mm[:, 2 * j:2 * j + 2, 0:HALF]

    def halves(t):
        return t.rearrange("p (a b) -> p a b", a=2)

    def bank(name, b):
        return ax[:, 2 * (USE[name] % 2) + b, :]

    def bank2(name):
        k = 2 * (USE[name] % 2)
        return ax[:, k:k + 2, 0:HALF]

    def sem(name):
        return ctx.enter_context(nc.semaphore(name))

    ln1_in = sem("ln1_in")
    c1_in, c2_in, vec_in, cache_in, rope_in, wg_in = map(sem, ("c1_in", "c2_in", "vec_in", "cache_in", "rope_in", "wg_in"))
    x_in = [sem(f"x_in{j}") for j in range(NJ + 1)]
    w0_in, w0_in2 = sem("w0_in"), sem("w0_in2")
    landed = [sem(f"landed{s}") for s in range(2)]
    hi_ready, lo_ready = sem("hi_ready"), sem("lo_ready")
    hi0_half, lo0_half = sem("hi0_half"), sem("lo0_half")
    filled = [sem(f"filled{j}") for j in range(2)]
    drained = [sem(f"drained{j}") for j in range(2)]
    aux_filled = [sem(f"aux_filled{j}") for j in range(2)]
    aux_drained = [sem(f"aux_drained{j}") for j in range(2)]
    down_part = sem("down_part")
    act_step, dve_step, pool_step = sem("act_step"), sem("dve_step"), sem("pool_step")
    n_hi, n_lo = sem("n_hi"), sem("n_lo")
    x_kept = sem("x_kept")
    sq8_done, acc1_done = sem("sq8_done"), sem("acc1_done")
    sq_done, acc_done = sem("sq_done"), sem("acc_done")
    rstd_ready = sem("rstd_ready")
    last_sq, last_fin, last_acc, last_sums, last_roots, last_rstd = map(
        sem, ("last_sq", "last_fin", "last_acc", "last_sums", "last_roots", "last_rstd"))
    ones_row, masks_clear = sem("ones_row"), sem("masks_clear")
    z_abs, ln_done, la_ready = sem("z_abs"), sem("ln_done"), sem("la_ready")
    b_gap, decays, qkd_ready = sem("b_gap"), sem("decays"), sem("qkd_ready")
    s0g_in, s0g_out, gst_out = map(sem, ("s0g_in", "s0g_out", "gst_out"))
    gvm_ready, rvm_ready = sem("gvm_ready"), sem("rvm_ready")
    qbs_ready = sem("qbs_ready")
    k3_high, k3_ready = sem("k3_high"), sem("k3_ready")
    osq_done, o_ready = sem("osq_done"), sem("o_ready")
    swapped, qk_ready = sem("swapped"), sem("qk_ready")
    dec_in = [sem(f"dec_in{i}") for i in range(2)]
    s0r_in = [sem(f"s0r_in{i}") for i in range(2)]
    s0r_out = [sem(f"s0r_out{i}") for i in range(2)]
    rst_out = sem("rst_out")
    silu_done, y_prod, y_hi, y_lo = map(sem, ("silu_done", "y_prod", "y_hi", "y_lo"))
    gate_done, m_sum, m_hi, m_lo = map(sem, ("gate_done", "m_sum", "m_hi", "m_lo"))
    ext_prev, ext_saved = sem("ext_prev"), sem("ext_saved")
    cb_first, conv_done, gelu_done, gl_scaled, g_hi, g_lo = map(
        sem, ("cb_first", "conv_done", "gelu_done", "gl_scaled", "g_hi", "g_lo"))
    fin_ready, conv_out, y_done, y_done_a, y_out, y_out_a = map(
        sem, ("fin_ready", "conv_out", "y_done", "y_done_a", "y_out", "y_out_a"))
    block = ctx.enter_context(nc.Block())

    HALVES = (slice(0, HALF), slice(HALF, NT))
    LAST = (KD - 2, KD - 1)

    def fills(j, u):
        return u + 1 if j == 1 or u < 2 else u

    F0 = [fills(j, U_GATE - 1) for j in range(2)]
    FW = [n + 16 for n in F0]
    FU = [n + 4 for n in FW]
    FD = [n + KF for n in FU]

    def aux_wait_filled(eng, name):
        k = USE[name]
        eng.wait_ge(aux_filled[k % 2], k // 2 + 1)

    def aux_wait_drained(eng, name):
        k = USE[name]
        eng.wait_ge(aux_drained[k % 2], k // 2 + 1)

    def aux_take(eng, name):
        k = USE[name]
        if k >= 2:
            eng.wait_ge(aux_drained[k % 2], k // 2)

    def filled_sem(name):
        return aux_filled[USE[name] % 2]

    def drained_sem(name):
        return aux_drained[USE[name] % 2]

    def gla_out(h):
        return gqk[:, h // 2 + 2 * (1 - h % 2), :]

    NORMS = [s for s in ORDER if s[0] in ("gn", "rn")]

    def normed(s):
        return gla_out(s[1]) if s[0] == "gn" else qk[:, s[1], :]

    def y_parts(n):
        h = n % HEADS
        return ysil[n], (HEADS + h if n < HEADS else h), \
            ("gn", h) if n < HEADS else ("rn", h)

    def vdst(h):
        big, small = (vg, vgs) if h < HEADS else (vr, vrs)
        c = (h % HEADS) * DV
        return big[:, :, c:c + DV], small[:, c:c + DV]

    @block.sync
    def _(sp):
        sp.dma_start(c1[:, :], A["c1"]).then_inc(c1_in, 16)
        sp.dma_start(x_smp[:, :], A["x_sample"].rearrange("b t d -> (b t) d")).then_inc(x_in[NJ], 16)
        xp = A["x_prompt"][0].rearrange("(j p) d -> p j d", p=P)
        for j in range(NJ):
            sp.dma_start(x_nat[:, j, :], xp[:, j, :]).then_inc(x_in[j], 16)

        w_in = A["w_in"][0].rearrange("(k p) n -> p k n", p=P)
        w_o = A["w_o"][0].rearrange("(k p) n -> p k n", p=P)
        w_up = A["w_up"][0].rearrange("(k p) n -> p k n", p=P)
        w_down = A["w_down"][0].rearrange("(k p) n -> p k n", p=P)
        w_ret = A["w_ret_out"][0].rearrange("(k p) n -> p k n", p=P)
        w_gla = A["w_gla_out"][0].rearrange("(k p) n -> p k n", p=P)

        def load(s, free, first, second, n1=4, n2=4):
            if free is not None:
                if not isinstance(free, int):
                    free = sp.snap(free)
                sp.wait_ge(lo_ready, free)
            sp.dma_start(raw[s][:, 0:n1, :], first).then_inc(landed[s], 16)
            sp.dma_start(raw[s][:, n1:n1 + n2, :], second).then_inc(landed[s], 16)

        def cols(w, c):
            return w[:, 0:4, bass.ds(c, UC)], w[:, 4:8, bass.ds(c, UC)]

        first, second = cols(w_in, HEAD_UNITS[0][1])
        sp.dma_start(raw[0][:, 0:4, :], first).then_inc(w0_in, 16)
        sp.dma_start(raw[0][:, 4:8, :], second).then_inc(w0_in2, 16)
        for u, (_, c) in enumerate(HEAD_UNITS[1:], 1):
            load(u % 2, u - 1 if u >= 2 else None, *cols(w_in, c))
        with sp.Fori(1, 3) as it:
            for n in range(6):
                u, q, kind = U_GATE + n, n // 3, n % 3
                free = it * 6 + (u - 7)
                if kind == 0:
                    load(u % 2, free, *cols(w_in, it * 512 + (MR + UC * q - 512)))
                elif kind == 1:
                    load(u % 2, free, *cols(w_in, it * 512 + (MG + UC * q - 512)))
                else:
                    c = bass.ds(it * 512 + (UC * q - 512), UC)
                    load(u % 2, free, w_ret[:, :, c], w_gla[:, :, c])
        with sp.Fori(1, 3) as it:
            for n in range(2):
                u = U_WO + n
                load(u % 2, it * 2 + (u - 3), *cols(w_o, it * 512 + (UC * n - 512)))
        with sp.Fori(1, KF // 2 + 1) as it:
            load(U_UP % 2, it * 2 + (U_UP - 3), *cols(w_up, it * UC - UC))
            load((U_UP + 1) % 2, it * 2 + (U_UP - 2), *cols(w_up, it * UC + (D_FF - UC)))
        with sp.Fori(1, 3) as it:
            for n in range(6):
                u, q, part = U_DOWN + n, n // 3, n % 3
                c = bass.ds(it * 512 + (UC * q - 512), UC)
                k0, n2 = 8 * part, 4 if part < 2 else 2
                load(u % 2, it * 6 + (u - 7), w_down[:, k0:k0 + 4, c], w_down[:, k0 + 4:k0 + 4 + n2, c], 4, n2)

        aux_wait_drained(sp, ("tail", 2))
        sp.dma_start(O[6][0, 0], tail_nat[0:2, :]).then_inc(conv_out, 16)
        sp.dma_start(O[7][0].rearrange("b r d -> (b r) d"), tail_nat[2:18, :]).then_inc(conv_out, 16)
        yp = O[0][0].rearrange("(j p) d -> p j d", p=P)
        for j in range(NJ - 1):
            sp.wait_ge(y_done, j + 1)
            sp.dma_start(yp[:, j, :], y_nat[:, j, :]).then_inc(y_out, 16)
        sp.wait_ge(y_done, NJ)
        sp.dma_start(O[1].rearrange("b t d -> (b t) d"), y_smp[:, :]).then_inc(y_out, 16)
        sp.wait_ge(conv_out, 32)
        sp.wait_ge(y_out, 16 * NJ)

    @block.gpsimd
    def _(pool):
        st = Steps(pool, pool_step)

        def spread(out, v3, v, h, ready, last_ready):
            x = v[:, h * DV:(h + 1) * DV]
            pool.wait_ge(*last_ready)
            st.did(pool.tensor_copy(v3[0:NS, :], x))
            st.wait()
            st.did(pool.tensor_copy(v3[2 * NS:3 * NS, :], x))
            st.wait()
            st.did(pool.tensor_tensor(v3[NS:2 * NS, :], x, v3[0:NS, :].bitcast(F32), ALU.subtract))
            st.wait()
            pool.tensor_tensor(out[:, :, :], v3[:, :].bitcast(F32).unsqueeze(1).to_broadcast([3 * NS, DEC_BATCH, DV]),
                               c2[0:3 * NS, C2_BM:C2_BM + DEC_BATCH].unsqueeze(2).to_broadcast([3 * NS, DEC_BATCH, DV]),
                               ALU.mult).then_inc(ready, 1)

        def key_low(step, keys, n, spread_ready):
            pool.wait_ge(k3_high, n)
            pool.wait_ge(*spread_ready)
            aux_wait_drained(pool, step)
            pool.tensor_tensor(k3[2 * NS:3 * NS, :], keys[:, :], k3[0:NS, :].bitcast(F32), ALU.subtract
                               ).then_inc(k3_ready, 1)
            pool.wait_ge(k3_ready, n)

        for off, name, n in ((V_LN1, "ln1", KD), (V_LN2, "ln2", KD), (V_GRET, "g_ret", HEADS), (V_GGLA, "g_gla", HEADS),
                             (V_CB, "conv_b", KF)):
            pool.dma_start(vrow[off:off + n, :], A[name][0].rearrange("(r p) -> r p", p=P)).then_inc(vec_in, 16)
        pool.dma_start(vrow[V_LNF:V_LNF + KD, :], A["ln_f"].rearrange("(r p) -> r p", p=P)).then_inc(vec_in, 16)
        pool.dma_start(vrow[V_CW:V_CW + 3 * KF, :], A["conv_w"][0].rearrange("i (r p) -> (i r) p", p=P)).then_inc(vec_in, 16)
        pool.dma_start(cache[:, :], A["cache_conv"][0].rearrange("b r d -> (b r) d")).then_inc(cache_in, 16)
        pool.dma_start(c2[:, :], A["c2"]).then_inc(c2_in, 16)
        pool.dma_start(cosT[:, :], A["rope"][:, 0, :]).then_inc(rope_in, 16)
        pool.dma_start(sinT[:, :], A["rope"][:, 1, :]).then_inc(rope_in, 16)
        pool.dma_start(wg[0:RANK, :], A["w_gate_up"][0]).then_inc(wg_in, 16)
        pool.dma_start(wg[RANK:RANK + 1, :], A["b_gate_up"]).then_inc(wg_in, 16)
        pool.memset(qbs[:, :, :], 0.0).then_inc(masks_clear, 1)
        pool.memset(ga[:, :], 1.0).then_inc(ones_row, 1)
        pool.wait_ge(rstd_ready, 1)
        for t in (*gsc, *gss):
            pool.memset(t[:], 0.0).then_inc(masks_clear, 1)

        for s in ORDER:
            if s[0] == "ex":
                p = s[1]
                if p == 0:
                    aux_wait_drained(pool, ("x", NJ - 1))
                    aux_wait_drained(pool, "cache")
                else:
                    pool.wait_ge(s0g_out, 16)
                    pool.dma_start(dec[0][:, :], A["decay"][:, 0, :]).then_inc(dec_in[0], 16)
                pool.dma_start(s0g[:, :, :], A["state_gla"][0, :, 2 * p:2 * p + 2].rearrange("b r c v -> (r c) b v")
                               ).then_inc(s0g_in, 16)
                if p == 0:
                    pool.wait_ge(c2_in, 16)
                    aux_wait_drained(pool, ("v", 0))
                    spread(gvm, gv3, vgs, 0, gvm_ready, (masks_clear, 5))
            elif s[0] == "kt":
                key_low(s, kts, s[1] + 1, (gvm_ready, 2 * s[1] + 1))
            elif s[0] == "gu":
                aux_wait_drained(pool, s)
                p = s[1]
                pool.dma_start(O[4][0, 0, 2 * p:2 * p + 2].rearrange("r c v -> (r c) v"), gst[:, p, NC - 1, :]
                               ).then_inc(gst_out, 16)
            elif s[0] == "gw":
                h = s[1]
                if h + 1 < HEADS:
                    aux_wait_filled(pool, s)
                    aux_wait_drained(pool, ("v", h + 1))
                    spread(gvm, gv3, vgs, h + 1, gvm_ready, (gvm_ready, h + 1))
                if h % 2 == 1:
                    aux_wait_drained(pool, s)
                    pool.dma_start(O[5][0, :, h - 1:h + 1].rearrange("b r c v -> (r c) b v"), s0g[:, :, :]
                                   ).then_inc(s0g_out, 16)
            elif s == ("v", 7):
                aux_wait_filled(pool, s)
                pool.dma_start(dec[1][:, :], A["decay"][:, 1, :]).then_inc(dec_in[1], 16)
            elif s[0] == "rk" and s[1] > 0:
                key_low(s, rks, 2 + s[1] + 1, (rvm_ready, s[1] + 1))
            elif s == ("rk", 0):
                pool.wait_ge(qk_ready, 8)
                for h in range(2):
                    pool.dma_start(s0r[h][:, :, :], A["state_ret"][0, :, h].rearrange("b c v -> c b v")
                                   ).then_inc(s0r_in[h], 16)
                aux_wait_filled(pool, ("gw", 3))
                key_low(s, rks, 3, (gvm_ready, HEADS))
                aux_wait_drained(pool, ("v", 4))
                spread(rvm, rv3, vrs, 0, rvm_ready, (gvm_ready, HEADS))
            elif s[0] == "rw":
                h = s[1]
                if h + 1 < HEADS:
                    aux_wait_filled(pool, s)
                    aux_wait_drained(pool, ("v", HEADS + h + 1))
                    spread(rvm, rv3, vrs, h + 1, rvm_ready, (rvm_ready, h + 1))
                aux_wait_drained(pool, s)
                pool.dma_start(O[3][0, :, h].rearrange("b c v -> c b v"), s0r[h % 2][:, :, :]
                               ).then_inc(s0r_out[h % 2], 16)
                if h + 2 < HEADS:
                    aux_wait_drained(pool, ("rs1", h))
                    pool.dma_start(dec[h % 2][:, :], A["decay"][:, h + 2, :]).then_inc(dec_in[h % 2], 16)
                    pool.wait_ge(s0r_out[h % 2], 16)
                    pool.dma_start(s0r[h % 2][:, :, :], A["state_ret"][0, :, h + 2].rearrange("b c v -> c b v")
                                   ).then_inc(s0r_in[h % 2], 16)
            elif s[0] == "rp":
                aux_wait_drained(pool, s)
                pool.dma_start(O[2][0, 0, s[1]], rst[:, :]).then_inc(rst_out, 16)

        with pool.Fori(0, KF // 2) as i:
            for j in range(2):
                t = i * 2 + j
                pool.wait_ge(conv_done, t + 1)
                pool.tensor_copy(seqs[:, :, 0:2].unsqueeze(1), pt[:, bass.ds(t, 1), 2:18].rearrange(
                    "p o (b t) -> p o b t", t=2)).then_inc(ext_prev, 1)
                pool.wait_ge(drained[j], i * 2 + FU[j] + 1)
                pool.wait_ge(ext_prev, t + 1)
                pool.tensor_copy(pt[:, bass.ds(t, 1), 0:2], ext[:, SEQ:SEQ + 2].unsqueeze(1)).then_inc(pool_step, 1)
                pool.tensor_copy(pt[:, bass.ds(t, 1), 2:18].rearrange("p o (b t) -> p o b t", t=2),
                                 seqs[:, :, DEC_SEQ:DEC_SEQ + 2].unsqueeze(1)).then_inc(ext_saved, 1)
            for j in range(2):
                pool.wait_ge(gelu_done, i * 2 + j + 1)
                pool.tensor_tensor(gl[j][:, :], gl[j][:, :], rstd[:, :], ALU.mult).then_inc(gl_scaled, 1)
        pool.wait_ge(gst_out, 32)
        pool.wait_ge(s0g_out, 32)
        pool.wait_ge(s0r_out[0], 32)
        pool.wait_ge(s0r_out[1], 32)
        pool.wait_ge(rst_out, 64)

    @block.scalar
    def _(act):
        st = Steps(act, act_step)

        def run(out, in_, func, done, **kw):
            return act.activation(out, in_, func, **kw).then_inc(done, 1)

        def hi(u, s, landed_count, slot_free=None):
            act.wait_ge(landed[s], landed_count - (32 if s == 0 else 0))
            if slot_free is not None:
                act.wait_ge(*slot_free)
            run(whi[s][:, :, :], raw[s][:, :, :], ACT.Copy, hi_ready)

        act.dma_start(lnrow[:, :], A["ln1"][0].rearrange("(r p) -> r p", p=P)).then_inc(ln1_in, 16)
        aux_wait_filled(act, "ln1")
        run(ln1[:, :], bank("ln1", 0)[:, 0:KD], ACT.Copy, drained_sem("ln1"))
        for j in range(NJ):
            aux_wait_filled(act, ("x", j))
            run(resid[:, 0:4, P * j:P * (j + 1)], bank(("x", j), 0).rearrange("p (f t) -> p f t", f=4), ACT.Copy, x_kept)
        act.wait_ge(w0_in, 16)
        run(whi[0][:, 0:4, :], raw[0][:, 0:4, :], ACT.Copy, hi0_half)
        def square(f, places):
            n = squares[0]
            if n > 1:
                act.wait_ge(acc_done, n - 1)
            run(places[n % 2][:, :], resid[:, f, :], ACT.Square, sq_done)
            squares[0] += 1

        squares = [0]

        def root(name, width):
            aux_wait_filled(act, name)
            run(halves(rstd[:, :]), bank2(name), ACT.Sqrt, drained_sem(name), scale=1.0 / width, bias=eps)

        norms = 0
        for s in ORDER:
            k = s[0]
            if k == "split":
                u = s[1]
                hi(u, u % 2, 32 * (u // 2 + 1), (filled[1], fills(1, u - 2)) if u >= 2 else None)
            elif k == "n1":
                aux_wait_drained(act, "ln1")
                aux_wait_drained(act, ("x", NJ - 1))
                act.wait_ge(x_kept, NJ)
                for f in range(KD):
                    run(nhi[:, f, :], resid[:, f, :], ACT.Copy, n_hi, scale=ln1[:, f:f + 1])
                    if f == 1:
                        act.wait_ge(w0_in2, 16)
                        run(whi[0][:, 4:8, :], raw[0][:, 4:8, :], ACT.Copy, hi_ready)
            elif k == "vec":
                aux_wait_filled(act, "vec")
                run(vecs[:, :], bank("vec", 0)[:, 0:NV], ACT.Copy, drained_sem("vec"))
            elif k == "cache":
                aux_wait_filled(act, "cache")
                run(pt[:, :, 2:18], bank("cache", 0)[:, 0:16 * KF].rearrange("p (f r) -> p f r", r=16), ACT.Copy,
                    drained_sem("cache"))
            elif k == "sq1":
                run(sq8[:, :, :], resid[:, :, :], ACT.Square, sq8_done)
            elif k == "mt" and s[1] < 2:
                _, u, j = s
                act.wait_ge(filled[j], fills(j, u))
                run(halves(gqk[:, 2 * u + j, :]), slot(j), ACT.Copy, drained[j])
            elif k == "rstd1":
                root("rstd1", D_MODEL)
            elif k == "v":
                aux_wait_filled(act, s)
                big, small = vdst(s[1])
                st.did(act.activation(big, bank(s, 0).rearrange("p (j v) -> p j v", j=NJ), ACT.Copy))
                run(small, bank(s, 1)[0:NS, 0:P], ACT.Copy, drained_sem(s))
            elif k == "la":
                aux_wait_filled(act, ("z",))
                zb = 2 * (USE[("z",)] % 2)
                run(az[:, :, :].rearrange("p (b j) c -> p b (j c)", b=2), ax[:, zb:zb + 2, :], ACT.Abs, z_abs)
                aux_wait_filled(act, ("zs",))
                run(azs[:, :], bank(("zs",), 0)[0:NS, 0:256], ACT.Abs, z_abs)
                act.wait_ge(z_abs, 2)
                st.did(act.activation(az[:, :, :], az[:, :, :], ACT.Exp, scale=-1.0))
                st.did(act.activation(azs[:, :], azs[:, :], ACT.Exp, scale=-1.0))
                st.wait()
                run(az[:, :, :], az[:, :, :], ACT.Ln, ln_done, bias=1.0)
                run(azs[:, :], azs[:, :], ACT.Ln, ln_done, bias=1.0)
            elif k == "ex":
                p = s[1]
                aux_wait_filled(act, ("b", p))
                st.did(act.activation(bcum[:, 0:SEQ], bank(("b", p), 0), ACT.Copy))
                run(bcum[:, SEQ:NT], bank(("b", p), 1)[:, 0:NS], ACT.Copy, drained_sem(("b", p)))
                if p == 1:
                    aux_wait_drained(act, ("gw", 1))
                    aux_wait_filled(act, ("gs", 1))
                aux_wait_drained(act, ("b", p))
                st.did(act.activation(ebp[:, :], bcum[:, :], ACT.Exp))
                st.did(act.activation(ebm[:, :], bcum[:, :], ACT.Exp, scale=-1.0))
                act.wait_ge(b_gap, p + 1)
                run(etl[:, :], etl[:, :], ACT.Exp, decays)
            elif k == "kt":
                p = s[1]
                aux_wait_filled(act, s)
                if p == 1:
                    aux_wait_filled(act, ("gw", 1))
                st.did(act.activation(ktn[:, :, :], bank(s, 0).rearrange("p (j c) -> p j c", j=NJ), ACT.Copy))
                st.did(act.activation(k3[0:NS, :], bank(s, 1)[0:NS, 0:P], ACT.Copy))
                run(k3[NS:2 * NS, :], bank(s, 1)[0:NS, 0:P], ACT.Copy, k3_high)
                run(kts[:, :], bank(s, 1)[0:NS, 0:P], ACT.Copy, drained_sem(s))
            elif k == "go":
                h = s[1]
                aux_wait_filled(act, s)
                run(gla_out(h)[:, 0:SEQ], bank(s, 0), ACT.Copy, drained_sem(s))
            elif k == "gx":
                aux_wait_filled(act, s)
                act.wait_ge(qbs_ready, 2 * s[1] + 2)
                st.did(act.activation(gla_out(2 * s[1])[:, SEQ:NT], bank(s, 0)[:, 0:NS], ACT.Copy))
                run(gla_out(2 * s[1] + 1)[:, SEQ:NT], bank(s, 0)[:, NS:2 * NS], ACT.Copy, drained_sem(s))
            elif k in ("gsq", "rsq"):
                aux_wait_drained(act, ("go" if k == "gsq" else "ro", s[1]))
                if k == "gsq":
                    aux_wait_drained(act, ("gx", s[1] // 2))
                n = NORMS.index(("gn" if k == "gsq" else "rn", s[1]))
                if n == 0:
                    act.wait_ge(qk_ready, 8)
                else:
                    aux_wait_filled(act, NORMS[n - 1])
                run(gsq[:, :], normed(NORMS[n]), ACT.Square, osq_done)
            elif k in ("gn", "rn"):
                aux_wait_filled(act, s)
                if norms > 0:
                    act.wait_ge(o_ready, norms)
                run(halves(grs[:, :]), bank2(s), ACT.Sqrt, drained_sem(s), scale=1.0 / DV, bias=eps)
                norms += 1
            elif k == "rope":
                i = s[1]
                act.wait_ge(drained[i % 2], fills(i % 2, 5 + i // 2))
                if i > 0:
                    act.wait_ge(qk_ready, i)
                half = RET_DK // 2
                st.did(act.activation(swp[0:half, :], qk[half:P, i, :], ACT.Copy))
                run(swp[half:P, :], qk[0:half, i, :], ACT.Copy, swapped)
            elif k == "ro":
                aux_wait_filled(act, s)
                st.did(act.activation(qk[:, s[1], 0:SEQ], bank(s, 0), ACT.Copy))
                run(qk[:, s[1], SEQ:NT], bank(s, 1)[:, 0:NS], ACT.Copy, drained_sem(s))
            elif k == "rp":
                aux_wait_filled(act, s)
                if s[1] > 0:
                    act.wait_ge(rst_out, 16 * s[1])
                run(rst[:, :], bank(s, 0)[:, 0:DV], ACT.Copy, drained_sem(s))
            elif k == "sl":
                n = s[1]
                u, j = 11 + n // 2, n % 2
                act.wait_ge(drained[j], fills(j, u))
                run(y_parts(n)[0][:, :], y_parts(n)[0][:, :], ACT.Silu, silu_done)
            elif k == "y2":
                n = s[1]
                if n == 0:
                    act.wait_ge(gst_out, 32)
                    act.wait_ge(s0g_out, 32)
                act.wait_ge(y_prod, n + 1)
                run(yhi[:, y_parts(n)[1], :], y_parts(n)[0][:, :], ACT.Copy, y_hi)

        with act.Fori(0, 2) as it:
            for n in range(6):
                q, kind = n // 3, n % 3
                u = U_GATE + n
                done = F0[1] + 4 * q + (1, 2, 4)[kind]
                for j in range(2):
                    if j == 1:
                        hi(u + 2, u % 2, it * 96 + 32 * (u // 2 + 2), (filled[1], it * 8 + done))
                    if kind < 2:
                        act.wait_ge(drained[j], it * 8 + F0[j] + 4 * q + kind + 1)
                        t = gsig[:, 2 * kind + j, :]
                        run(t, t, ACT.Sigmoid, gate_done)
                    else:
                        act.wait_ge(m_sum, it * 4 + 2 * q + j + 1)
                        run(mhi[:, bass.ds(it * 4 + 2 * q + j, 1), :].rearrange("p o t -> p (o t)"), mx[0][:, :],
                            ACT.Copy, m_hi)
        for n in range(4):
            u = U_WO + n
            for j in range(2):
                f = 2 * n + j
                act.wait_ge(drained[j], FW[j] + n + 1)
                run(nhi[:, f, :], resid[:, f, :], ACT.Copy, n_hi, scale=vec(V_LN2 + f))
                square(f, hsq)
            hi(u + 2, u % 2, 32 * (u // 2 + 2), (filled[1], FW[1] + n + 1))
        root("rstd2", D_MODEL)
        with act.Fori(0, KF // 2) as i:
            for j in range(2):
                t = i * 2 + j
                act.wait_ge(drained[j], i * 2 + FU[j] + 1)
                act.wait_ge(ext_prev, t + 1)
                if j == 1:
                    act.wait_ge(gelu_done, t)
                run(cb[:, 0:CONV], ext[:, 0:CONV], ACT.Identity, cb_first, scale=vecs[:, bass.ds(t + V_CW, 1)],
                    bias=vecs[:, bass.ds(t + V_CB, 1)])
                if j == 1:
                    u = U_UP
                    hi(u + 2, u % 2, i * 32 + 32 * (u // 2 + 2), (filled[1], i * 2 + FU[1] + 1))
                act.wait_ge(conv_done, t + 2)
                st.did(act.activation(gl[j][:, 0:SEQ], cb[:, 0:SEQ], ACT.Gelu))
                run(gl[j][:, SEQ:NT].rearrange("p (b t) -> p b t", t=DEC_SEQ), conv_seqs, ACT.Gelu, gelu_done)
            for j in range(2):
                t = i * 2 + j
                if j == 1:
                    u = U_UP + 1
                    hi(u + 2, u % 2, i * 32 + 32 * (u // 2 + 2), (filled[1], i * 2 + FU[1] + 2))
                act.wait_ge(drained[j], i * 2 + FU[j] + 2)
                run(ghi[:, bass.ds(t, 1), :].rearrange("p o t -> p (o t)"), gl[j][:, :], ACT.Copy, g_hi)
        st.n += 2 * (KF // 2 - 1)
        def tail_rows():
            for i in range(3):
                aux_wait_filled(act, ("tail", i))
                t0, n = 8 * i, min(8, KF - 8 * i)
                b = 2 * (USE[("tail", i)] % 2)
                run(tail_nat[:, P * t0:P * (t0 + n)], ax[0:18, b:b + 2, :].rearrange("p a b -> p (a b)")[:, 0:P * n],
                    ACT.Copy, drained_sem(("tail", i)))

        def y_rows(*tiles):
            for f in tiles:
                aux_wait_filled(act, ("y", f))
                st.did(act.activation(y_nat[:, :, P * f:P * (f + 1)], bank(("y", f), 0).rearrange("p (j c) -> p j c", j=NJ),
                                      ACT.Copy))
                run(y_smp[:, P * f:P * (f + 1)], bank(("y", f), 1)[0:NS, 0:P], ACT.Copy, drained_sem(("y", f)))

        for q in range(4):
            for part in range(3):
                u = U_DOWN + 3 * q + part
                if part == 2 and q < 3:
                    for j in range(2):
                        f = 2 * q + j
                        act.wait_ge(drained[j], FD[j] + q + 1)
                        if f >= 2:
                            aux_wait_filled(act, ("y", f - 2))
                        run(fin[j][:, :], resid[:, f, :], ACT.Copy, fin_ready, scale=vec(V_LNF + f))
                        square(f, osq)
                if (q, part) == (0, 0):
                    tail_rows()
                if u + 2 < U_END:
                    after = ((down_part, 2 * q + 1), (down_part, 2 * q + 2), (filled[1], FD[1] + q + 1))[part]
                    hi(u + 2, u % 2, 32 * (u // 2 + 2), after)
                if part == 0 and q > 0:
                    y_rows(2 * q - 2, 2 * q - 1)
                if (q, part) == (3, 1):
                    st.did(act.activation(rstd_col[:, NJ + 1:NJ + 2], eps, ACT.Sqrt))

        def last_tile(e, j):
            act.wait_ge(drained[j], FD[j] + 4 + e)
            if e == 0:
                act.wait_ge(acc_done, 2 * KD - 3 + j)
                aux_wait_filled(act, ("y", KD - 4 + j))
            t = HALVES[e]
            run(osq[j][:, t], resid[:, LAST[j], t], ACT.Square, last_sq)
            run(fin[j][:, t], resid[:, LAST[j], t], ACT.Copy, last_fin, scale=vec(V_LNF + LAST[j]))

        def last_rows(e):
            name, b = ("ye", e), mm[:, e, :]
            act.wait_ge(last_sums, e + 1)
            run(rstd_col[:, 2 * e:2 * e + 2], b[:, 2 * e:2 * e + 2], ACT.Sqrt, last_roots, scale=1.0 / D_MODEL, bias=eps)
            if e == 1:
                run(rstd_col[0:NS, NJ:NJ + 1], b[0:NS, NJ:NJ + 1], ACT.Sqrt, last_roots, scale=1.0 / D_MODEL,
                    bias=eps[0:NS])
            aux_wait_filled(act, name)
            out = y_nat[:, 2 * e:2 * e + 2, P * LAST[0]:].rearrange("p j (f c) -> p f j c", f=2)
            ins = act.activation(out, bank(name, 0).rearrange("p (f j c) -> p f j c", f=2, j=2), ACT.Copy)
            if e == 0:
                ins.then_inc(drained_sem(name), 1)
            else:
                st.did(ins)
                run(y_smp[:, P * LAST[0]:], bank(name, 1)[0:NS, 0:2 * P], ACT.Copy, drained_sem(name))

        last_tile(0, 0)
        last_tile(0, 1)
        last_tile(1, 0)
        last_rows(0)
        last_tile(1, 1)
        last_rows(1)
        act.wait_ge(last_rstd, 2)
        aux_wait_drained(act, ("ye", 1))
        j = NJ - 1
        run(y_nat[:, j, :], y_nat[:, j, :], ACT.Copy, y_done_a, scale=rstd_col[:, j:j + 1])
        act.wait_ge(y_done_a, 1)
        act.dma_start(O[0][0].rearrange("(j p) d -> p j d", p=P)[:, j, :], y_nat[:, j, :]).then_inc(y_out_a, 16)
        act.wait_ge(y_out_a, 16)

    @block.vector
    def _(dve):
        st = Steps(dve, dve_step)

        def lo(u, s, count):
            dve.wait_ge(hi_ready, count)
            dve.tensor_tensor(wlo[s][:, :, :], raw[s][:, :, :], whi[s][:, :, :].bitcast(F32), ALU.subtract
                              ).then_inc(lo_ready, 1)

        def scaled(out, j, count):
            dve.wait_ge(filled[j], count)
            dve.tensor_tensor(halves(out), slot(j), halves(rstd[:, :]), ALU.mult).then_inc(drained[j], 1)

        def inverse(out, name, done):
            aux_wait_drained(dve, name)
            dve.reciprocal(out, out).then_inc(done, 1)

        adds = [0]

        def add_square(out, places, first):
            n = adds[0]
            dve.wait_ge(sq_done, n + 1)
            if first:
                dve.tensor_copy(out[:, :], places[n % 2][:, :]).then_inc(acc_done, 1)
            else:
                dve.wait_ge(acc_done, n)
                dve.tensor_tensor(out[:, :], out[:, :], places[n % 2][:, :], ALU.add).then_inc(acc_done, 1)
            adds[0] += 1

        aux_wait_filled(dve, ("x", NJ))
        dve.tensor_copy(resid[:, :, SEQ:NT], bank(("x", NJ), 0)[:, 0:KD * NS].rearrange("p (f t) -> p f t", f=KD)
                        ).then_inc(drained_sem(("x", NJ)), 1)
        for j in range(NJ):
            aux_wait_filled(dve, ("x", j))
            dve.tensor_copy(resid[:, 4:8, P * j:P * (j + 1)], bank(("x", j), 1).rearrange("p (f t) -> p f t", f=4)
                            ).then_inc(drained_sem(("x", j)), 1)
        norms = 0
        for s in ORDER:
            k = s[0]
            if k == "split":
                lo(s[1], s[1] % 2, s[1] + 1)
            elif k == "n1":
                dve.wait_ge(hi0_half, 1)
                dve.tensor_tensor(wlo[0][:, 0:4, :], raw[0][:, 0:4, :], whi[0][:, 0:4, :].bitcast(F32), ALU.subtract
                                  ).then_inc(lo0_half, 1)
                aux_wait_drained(dve, "ln1")
                aux_wait_drained(dve, ("x", NJ - 1))
                dve.wait_ge(x_kept, NJ)
                for f in range(KD):
                    dve.wait_ge(n_hi, f + 1)
                    dve.scalar_tensor_tensor(nlo[:, f, :], resid[:, f, :], ln1[:, f:f + 1], nhi[:, f, :].bitcast(F32),
                                             op0=ALU.mult, op1=ALU.subtract).then_inc(n_lo, 1)
                    if f == 1:
                        dve.wait_ge(hi_ready, 1)
                        dve.tensor_tensor(wlo[0][:, 4:8, :], raw[0][:, 4:8, :], whi[0][:, 4:8, :].bitcast(F32),
                                          ALU.subtract).then_inc(lo_ready, 1)
            elif k == "sq1":
                dve.wait_ge(sq8_done, 1)
                st.did(dve.tensor_tensor(sq8[:, 0:4, :], sq8[:, 0:4, :], sq8[:, 4:8, :], ALU.add))
                st.wait()
                st.did(dve.tensor_tensor(sq8[:, 0:2, :], sq8[:, 0:2, :], sq8[:, 2:4, :], ALU.add))
                st.wait()
                dve.tensor_tensor(acc[:, :], sq8[:, 0, :], sq8[:, 1, :], ALU.add).then_inc(acc1_done, 1)
            elif k == "rstd1":
                inverse(rstd[:, :], "rstd1", rstd_ready)
                dve.wait_ge(rstd_ready, 1)
            elif k == "sc":
                for j in range(2):
                    dve.wait_ge(drained[j], fills(j, 1))
                st.did(dve.tensor_tensor(gqk[:, :, :], gqk[:, :, :], rstd[:, :].unsqueeze(1).to_broadcast([P, 4, NT]),
                                         ALU.mult))
            elif k == "mt" and s[1] >= 2:
                _, u, j = s
                kind, n = HEAD_UNITS[u][0], fills(j, u)
                if kind == "ga":
                    dve.wait_ge(ones_row, 1)
                    dve.wait_ge(filled[1], n)
                    dve.tensor_tensor(halves(ga[0:RANK, :]), slot(1)[0:RANK], halves(rstd[0:RANK, :]), ALU.mult
                                      ).then_inc(drained[1], 1)
                elif kind in ("gv", "rv"):
                    h = 2 * (u - 3) + j if kind == "gv" else HEADS + 2 * (u - 9) + j
                    if h >= 2:
                        aux_wait_filled(dve, ("v", h - 2))
                    scaled(vst[h % 2][:, :], j, n)
                elif kind in ("gg", "rg"):
                    y = 2 * (u - 11) + j
                    if y == 0:
                        aux_wait_filled(dve, ("gw", 3))
                        dve.wait_ge(gst_out, 32)
                    if y >= HEADS:
                        dve.wait_ge(y_prod, y - HEADS + 1)
                    scaled(y_parts(y)[0][:, :], j, n)
                else:
                    scaled(qk[:, 2 * (u - 5) + j, :], j, n)
            elif k == "la":
                dve.wait_ge(z_abs, 2)
                zb = 2 * (USE[("z",)] % 2)
                dve.tensor_scalar(la[:, :, :].rearrange("p (b j) c -> p b (j c)", b=2), ax[:, zb:zb + 2, :], 0.0, None,
                                  ALU.min).then_inc(drained_sem(("z",)), 1)
                dve.tensor_scalar(las[:, :], bank(("zs",), 0)[0:NS, 0:256], 0.0, None, ALU.min
                                  ).then_inc(drained_sem(("zs",)), 1)
                dve.wait_ge(ln_done, 2)
                aux_wait_drained(dve, ("zs",))
                aux_wait_drained(dve, ("z",))
                dve.tensor_tensor(la[:, :, :], la[:, :, :], az[:, :, :], ALU.subtract).then_inc(la_ready, 1)
                dve.tensor_tensor(las[:, :], las[:, :], azs[:, :], ALU.subtract).then_inc(la_ready, 1)
            elif k == "ex":
                p = s[1]
                aux_wait_drained(dve, ("b", p))
                if p == 1:
                    aux_wait_filled(dve, ("kt", 0))
                for a, b, c in ((0, SEQ, CHUNK), (SEQ, NT, DEC_SEQ)):
                    v = bcum[:, a:b].rearrange("p (n c) -> p n c", c=c)
                    w = etl[:, a:b].rearrange("p (n c) -> p n c", c=c)
                    ins = dve.tensor_tensor(w, v[:, :, c - 1:c].to_broadcast([P, (b - a) // c, c]), v, ALU.subtract)
                    if a == 0:
                        st.did(ins)
                    else:
                        ins.then_inc(b_gap, 1)
                dve.wait_ge(decays, p + 1)
                st.wait()
                st.did(dve.scalar_tensor_tensor(gqk[:, p, :], gqk[:, p, :], GLA_DK ** -0.5, ebp[:, :], op0=ALU.mult,
                                                op1=ALU.mult))
                st.did(dve.tensor_tensor(ebm[:, :], gqk[:, 2 + p, :], ebm[:, :], ALU.mult))
                dve.tensor_tensor(etl[:, :], gqk[:, 2 + p, :], etl[:, :], ALU.mult).then_inc(qkd_ready, 1)
                dve.wait_ge(masks_clear, 5)
                dve.wait_ge(qkd_ready, p + 1)
                if p == 1:
                    aux_wait_filled(dve, ("gx", 0))
                for h in range(2):
                    r = slice(GLA_DK * h, GLA_DK * (h + 1))
                    dve.tensor_copy(qbs[r, h, :], gqk[r, p, SEQ:NT]).then_inc(qbs_ready, 1)
            elif k == "gs":
                h = s[1]
                dve.wait_ge(masks_clear, 5)
                dve.wait_ge(c2_in, 16)
                aux_wait_filled(dve, s)
                if h >= 2:
                    aux_wait_filled(dve, ("go", h - 2))
                causal = c2[:, C2_U:C2_U + P].bitcast(U32).unsqueeze(1).to_broadcast([P, NJ, P])
                st.did(dve.copy_predicated(gsc[h % 2][:, :, :], causal, bank(s, 0).rearrange("p (j i) -> p j i", j=NJ)))
                dve.copy_predicated(gss[h % 2][:, :], c2[0:NS, C2_U4:C2_U4 + NS].bitcast(U32), bank(s, 1)[0:NS, 0:NS]
                                    ).then_inc(drained_sem(s), 1)
            elif k == "gu":
                p = s[1]
                aux_wait_filled(dve, s)
                for c in range(NC):
                    new = bank(s, c % 2)[:, (c // 2) * DV:(c // 2 + 1) * DV]
                    if c == 0:
                        st.did(dve.tensor_copy(gst[:, p, 0, :], new))
                        continue
                    st.wait()
                    last = CHUNK * (c + 1) - 1
                    ins = dve.scalar_tensor_tensor(gst[:, p, c, :], gst[:, p, c - 1, :], ebp[:, last:last + 1], new,
                                                   op0=ALU.mult, op1=ALU.add)
                    if c < NC - 1:
                        st.did(ins)
                    else:
                        ins.then_inc(drained_sem(s), 1)
            elif k == "gw":
                h = s[1]
                r = slice(GLA_DK * (h % 2), GLA_DK * (h % 2) + GLA_DK)
                aux_wait_filled(dve, s)
                end = ebp[r, SEQ + DEC_SEQ - 1:NT:DEC_SEQ].unsqueeze(2).to_broadcast([GLA_DK, DEC_BATCH, DV])
                st.did(dve.tensor_tensor(s0g[r, :, :], s0g[r, :, :], end, ALU.mult))
                st.wait()
                b = 2 * (USE[s] % 2)
                dve.tensor_tensor(s0g[r, :, :].rearrange("p (a b) v -> p a (b v)", a=2), ax[r, b:b + 2, :],
                                  s0g[r, :, :].rearrange("p (a b) v -> p a (b v)", a=2), ALU.add
                                  ).then_inc(drained_sem(s), 1)
            elif k in ("gi", "ri"):
                s = ("gn" if k == "gi" else "rn", s[1])
                inverse(grs[:, :], s, dve_step)
                st.n += 1
                st.wait()
                h = s[1]
                norms += 1
                dve.scalar_tensor_tensor(normed(s), normed(s), vec((V_GGLA if k == "gi" else V_GRET) + h), grs[:, :],
                                         op0=ALU.mult, op1=ALU.mult).then_inc(o_ready, 1)
            elif k == "rope":
                i = s[1]
                if i == 0:
                    dve.wait_ge(rope_in, 32)
                dve.wait_ge(swapped, i + 1)
                dve.wait_ge(drained[i % 2], fills(i % 2, 5 + i // 2))
                st.did(dve.tensor_tensor(rsn[:, :], swp[:, :], sinT[:, :], ALU.mult))
                st.did(dve.tensor_tensor(qk[:, i, :], qk[:, i, :], cosT[:, :], ALU.mult))
                st.wait()
                dve.tensor_tensor(qk[:, i, :], qk[:, i, :], rsn[:, :], ALU.add).then_inc(qk_ready, 1)
            elif k == "rk":
                h = s[1]
                aux_wait_filled(dve, s)
                aux_wait_filled(dve, ("rp", h - 1) if h else ("gw", 3))
                tail = c2[:, C2_TL + h:C2_TL + 4 * NJ:HEADS].unsqueeze(2).to_broadcast([P, NJ, P])
                st.did(dve.tensor_tensor(rkn[:, :, :], bank(s, 0).rearrange("p (j c) -> p j c", j=NJ), tail, ALU.mult))
                tail = c2[0:NS, C2_TLS + h:C2_TLS + h + 1]
                st.did(dve.tensor_scalar(k3[0:NS, :], bank(s, 1)[0:NS, 0:P], tail, None, ALU.mult))
                dve.tensor_scalar(k3[NS:2 * NS, :], bank(s, 1)[0:NS, 0:P], tail, None, ALU.mult).then_inc(k3_high, 1)
                dve.tensor_scalar(rks[:, :], bank(s, 1)[0:NS, 0:P], tail, None, ALU.mult).then_inc(drained_sem(s), 1)
            elif k == "rs0":
                h = s[1]
                dve.wait_ge(dec_in[h % 2], 16 * (h // 2 + 1))
                aux_wait_filled(dve, s)
                aux_wait_filled(dve, ("ro", h - 1) if h else ("go", 3))
                st.did(dve.tensor_tensor(rsc[:, 0:SEQ], bank(s, 0), dec[h % 2][:, :], ALU.mult))
                dve.tensor_tensor(rsc[:, RS0[1]:RS0[2]], bank(s, 1)[:, 0:SEQ - P], dec[h % 2][:, 0:SEQ - P], ALU.mult
                                  ).then_inc(drained_sem(s), 1)
            elif k == "rs1":
                h = s[1]
                st.did(dve.tensor_tensor(rqs[:, :], qk[:, h, SEQ:NT], c2[:, C2_QD + NS * h:C2_QD + NS * (h + 1)], ALU.mult))
                aux_wait_filled(dve, s)
                st.did(dve.tensor_tensor(rsc[:, RS0[2]:RS0[3]], bank(s, 0)[:, 0:2 * P], dec[h % 2][:, 0:2 * P], ALU.mult))
                st.did(dve.tensor_tensor(rsc[:, RS0[3]:], bank(s, 0)[:, 2 * P:3 * P], dec[h % 2][:, 0:P], ALU.mult))
                dve.tensor_tensor(rss[:, :], bank(s, 1)[0:NS, 0:NS], c2[0:NS, C2_DS + NS * h:C2_DS + NS * (h + 1)],
                                  ALU.mult).then_inc(drained_sem(s), 1)
            elif k == "rw":
                h = s[1]
                aux_wait_filled(dve, s)
                b = 2 * (USE[s] % 2)
                t = s0r[h % 2][:, :, :].rearrange("p (a b) v -> p a (b v)", a=2)
                dve.scalar_tensor_tensor(t, t, gamma4(h), ax[:, b:b + 2, :], op0=ALU.mult, op1=ALU.add
                                         ).then_inc(drained_sem(s), 1)
            elif k == "y1":
                n = s[1]
                t, _, norm = y_parts(n)
                dve.wait_ge(silu_done, n + 1)
                dve.wait_ge(o_ready, NORMS.index(norm) + 1)
                dve.tensor_tensor(t[:, :], t[:, :], normed(norm), ALU.mult).then_inc(y_prod, 1)
            elif k == "y2":
                n = s[1]
                t, y, _ = y_parts(n)
                dve.wait_ge(y_hi, n + 1)
                dve.tensor_tensor(ylo[:, y, :], t[:, :], yhi[:, y, :].bitcast(F32), ALU.subtract).then_inc(y_lo, 1)

        dve.wait_ge(rst_out, 16 * HEADS)
        with dve.Fori(0, 2) as it:
            for n in range(6):
                q, kind = n // 3, n % 3
                u = U_GATE + n
                for j in range(2):
                    if kind < 2:
                        if kind == 0:
                            dve.wait_ge(drained[1], it * 8 + F0[1] + 4 * q)
                        scaled(gsig[:, 2 * kind + j, :], j, it * 8 + F0[j] + 4 * q + kind + 1)
                        continue
                    m = it * 4 + 2 * q + j
                    for b in range(2):
                        dve.wait_ge(gate_done, it * 8 + 4 * q + 3 + j)
                        dve.wait_ge(filled[b], it * 8 + F0[b] + 4 * q + 3 + j)
                        if b == 0:
                            dve.wait_ge(*((m_lo, m) if j else (lo_ready, it * 6 + (u + 1))))
                        dve.tensor_tensor(halves(mx[b][:, :]), slot(b), halves(gsig[:, 2 * b + j, :]), ALU.mult
                                          ).then_inc(drained[b], 1)
                    for b in range(2):
                        dve.wait_ge(drained[b], it * 8 + F0[b] + 4 * q + 3 + j)
                    dve.tensor_tensor(mx[0][:, :], mx[0][:, :], mx[1][:, :], ALU.add).then_inc(m_sum, 1)
                    dve.wait_ge(m_hi, m + 1)
                    dve.tensor_tensor(mlo[:, bass.ds(m, 1), :].rearrange("p o t -> p (o t)"), mx[0][:, :],
                                      mhi[:, bass.ds(m, 1), :].rearrange("p o t -> p (o t)").bitcast(F32), ALU.subtract
                                      ).then_inc(m_lo, 1)
                lo(u + 2, u % 2, it * 6 + (u + 3))
        for n in range(4):
            u = U_WO + n
            for j in range(2):
                f = 2 * n + j
                dve.wait_ge(filled[j], FW[j] + n + 1)
                dve.tensor_tensor(halves(resid[:, f, :]), slot(j), halves(resid[:, f, :]), ALU.add).then_inc(drained[j], 1)
                dve.wait_ge(n_hi, KD + f + 1)
                dve.wait_ge(drained[j], FW[j] + n + 1)
                dve.scalar_tensor_tensor(nlo[:, f, :], resid[:, f, :], vec(V_LN2 + f), nhi[:, f, :].bitcast(F32),
                                         op0=ALU.mult, op1=ALU.subtract).then_inc(n_lo, 1)
                add_square(acc, hsq, f == 0)
            lo(u + 2, u % 2, u + 3)
        inverse(rstd[:, :], "rstd2", rstd_ready)
        dve.memset(ext[:, 0:2], 0.0).then_inc(conv_done, 1)
        dve.wait_ge(rstd_ready, 2)
        with dve.Fori(0, KF // 2) as i:
            st.off = i * 6
            for j in range(2):
                t = i * 2 + j
                dve.wait_ge(conv_done, t + 1)
                dve.wait_ge(ext_prev, t + 1)
                dve.wait_ge(filled[j], i * 2 + FU[j] + 1)
                st.did(dve.tensor_tensor(ext[:, 2:2 + HALF], mm[:, 2 * j, 0:HALF], rstd[:, 0:HALF], ALU.mult))
                st.did(dve.tensor_tensor(ext[:, 2 + HALF:2 + SEQ], mm[:, 2 * j + 1, 0:SEQ - HALF], rstd[:, HALF:SEQ],
                                         ALU.mult))
                dve.tensor_tensor(seqs[:, :, 2:2 + DEC_SEQ],
                                  mm[:, 2 * j + 1, SEQ - HALF:HALF].rearrange("p (b t) -> p b t", t=DEC_SEQ),
                                  rstd[:, SEQ:NT].rearrange("p (b t) -> p b t", t=DEC_SEQ), ALU.mult
                                  ).then_inc(drained[j], 1)
                dve.wait_ge(drained[j], i * 2 + FU[j] + 1)
                dve.wait_ge(cb_first, t + 1)
                st.did(dve.scalar_tensor_tensor(cb[:, 0:CONV], ext[:, 1:1 + CONV], vecs[:, bass.ds(t + (V_CW + KF), 1)],
                                                cb[:, 0:CONV], op0=ALU.mult, op1=ALU.add))
                st.wait()
                dve.scalar_tensor_tensor(cb[:, 0:CONV], ext[:, 2:2 + CONV], vecs[:, bass.ds(t + (V_CW + 2 * KF), 1)],
                                         cb[:, 0:CONV], op0=ALU.mult, op1=ALU.add).then_inc(conv_done, 1)
            u = U_UP
            lo(u + 2, u % 2, i * 2 + (u + 3))
            for j in range(2):
                t = i * 2 + j
                dve.wait_ge(gl_scaled, t + 1)
                dve.wait_ge(filled[j], i * 2 + FU[j] + 2)
                dve.tensor_tensor(halves(gl[j][:, :]), slot(j), halves(gl[j][:, :]), ALU.mult).then_inc(drained[j], 1)
                if j == 1:
                    u = U_UP + 1
                    lo(u + 2, u % 2, i * 2 + (u + 3))
                dve.wait_ge(drained[j], i * 2 + FU[j] + 2)
                dve.wait_ge(g_hi, t + 1)
                dve.tensor_tensor(glo[:, bass.ds(t, 1), :].rearrange("p o t -> p (o t)"), gl[j][:, :],
                                  ghi[:, bass.ds(t, 1), :].rearrange("p o t -> p (o t)").bitcast(F32), ALU.subtract
                                  ).then_inc(g_lo, 1)
        st.off, st.n = 0, st.n + 6 * (KF // 2 - 1)
        for q in range(4):
            for part in range(3):
                u = U_DOWN + 3 * q + part
                if part == 2 and q < 3:
                    for j in range(2):
                        f = 2 * q + j
                        dve.wait_ge(filled[j], FD[j] + q + 1)
                        dve.tensor_tensor(halves(resid[:, f, :]), slot(j), halves(resid[:, f, :]), ALU.add
                                          ).then_inc(drained[j], 1)
                        add_square(facc, osq, f == 0)
                if u + 2 < U_END:
                    lo(u + 2, u % 2, u + 3)

        def last_tile(e, j):
            t = HALVES[e]
            dve.wait_ge(filled[j], FD[j] + 4 + e)
            dve.tensor_tensor(resid[:, LAST[j], t], mm[:, 2 * j + e, 0:HALF], resid[:, LAST[j], t], ALU.add
                              ).then_inc(drained[j], 1)

        def last_squares(e):
            dve.wait_ge(last_sq, 2 * e + 1)
            dve.wait_ge(acc_done, 2 * KD - 2)
            dve.tensor_tensor(facc[:, HALVES[e]], facc[:, HALVES[e]], osq[0][:, HALVES[e]], ALU.add).then_inc(last_acc, 1)

        def factors(e):
            dve.wait_ge(last_roots, 1 if e == 0 else 3)
            ins = dve.reciprocal(rstd_col[:, 2 * e:2 * e + 2], rstd_col[:, 2 * e:2 * e + 2])
            if e == 0:
                ins.then_inc(last_rstd, 1)
            else:
                st.did(ins)
                dve.reciprocal(rstd_col[0:NS, NJ:NJ + 1], rstd_col[0:NS, NJ:NJ + 1]).then_inc(last_rstd, 1)
            dve.wait_ge(last_rstd, e + 1)
            aux_wait_drained(dve, ("ye", e))

        def scale_rows(y, col):
            dve.tensor_scalar(y, y, col, None, ALU.mult).then_inc(y_done, 1)

        last_tile(0, 0)
        last_tile(0, 1)
        last_squares(0)
        last_tile(1, 0)
        last_squares(1)
        factors(0)
        scale_rows(y_nat[:, 0, :], rstd_col[:, 0:1])
        last_tile(1, 1)
        scale_rows(y_nat[:, 1, :], rstd_col[:, 1:2])
        factors(1)
        scale_rows(y_nat[:, 2, :], rstd_col[:, 2:3])
        scale_rows(y_smp[:, :], rstd_col[0:NS, NJ:NJ + 1])

    @block.tensor
    def _(pe):
        def product(j, s, jj, ks, xh, xl, first=True, last=True, ready=None, banks=(0, 1)):
            for n, (kw, kx) in enumerate(ks):
                if ready:
                    ready(kx)
                c = slice(P * jj, P * (jj + 1))
                wh, wl = whi[s][:, kw, c], wlo[s][:, kw, c]
                for m, (w, x) in enumerate(((wh, xh), (wh, xl), (wl, xh))):
                    for a in banks:
                        ins = pe.matmul(mm[:, 2 * j + a, 0:HALF], w, x[:, kx, HALF * a:HALF * (a + 1)],
                                        start=first and n == 0 and m == 0, stop=last and n == len(ks) - 1 and m == 2)
            return ins

        every = [(k, k) for k in range(KD)]

        def small(out, w, x, start=True, stop=True, done=None):
            ins = pe.matmul(out, w, x, start=start, stop=stop, skip_group_check=True)
            if done is not None:
                ins.then_inc(done, 1)

        def turn(out, in_, done=None):
            ins = pe.transpose(out, in_, ident[0:in_.shape[0], 0:in_.shape[0]])
            if done is not None:
                ins.then_inc(done, 1)

        def turn_tokens(name, src):
            aux_take(pe, name)
            for j in range(NJ):
                turn(bank(name, 0)[:, P * j:P * (j + 1)], src[:, P * j:P * (j + 1)])
            turn(bank(name, 1)[0:NS, 0:P], src[:, SEQ:NT], filled_sem(name))

        def summed(name, sq):
            aux_take(pe, name)
            for a in range(2):
                small(bank(name, a)[:, 0:HALF], ones, sq[:, HALF * a:HALF * (a + 1)],
                      done=filled_sem(name) if a else None)

        pe.wait_ge(c1_in, 16)
        pe.wait_ge(ln1_in, 16)
        aux_take(pe, "ln1")
        turn(bank("ln1", 0)[:, 0:KD], lnrow[:, :], filled_sem("ln1"))
        for j in (NJ, *range(NJ)):
            pe.wait_ge(x_in[j], 16)
            aux_take(pe, ("x", j))
            if 2 <= j < NJ:
                pe.wait_ge(x_kept, j - 1)
            for f in range(KD):
                done = filled_sem(("x", j)) if f == KD - 1 else None
                if j < NJ:
                    turn(bank(("x", j), f // 4)[:, P * (f % 4):P * (f % 4 + 1)], x_nat[:, j, P * f:P * (f + 1)], done)
                else:
                    turn(bank(("x", j), 0)[:, NS * f:NS * (f + 1)], x_smp[:, P * f:P * (f + 1)], done)

        for s in ORDER:
            k = s[0]
            if k == "mt":
                _, u, j = s
                kind, n = HEAD_UNITS[u][0], fills(j, u)
                def ready_0(kx):
                    pe.wait_ge(n_lo, kx + 1)
                    if kx == 0:
                        pe.wait_ge(lo0_half, 1)
                    elif kx == 4:
                        pe.wait_ge(lo_ready, 1)

                ready = ready_0 if (u, j) == (0, 0) else None
                if ready is None:
                    pe.wait_ge(lo_ready, u + 1)
                if n >= 2:
                    pe.wait_ge(drained[j], n - 1)
                product(j, u % 2, 0 if kind == "ga" else j, every, nhi, nlo, ready=ready).then_inc(filled[j], 1)
            elif k == "vec":
                pe.wait_ge(vec_in, 112)
                aux_take(pe, "vec")
                turn(bank("vec", 0)[:, 0:NV], vrow[:, :], filled_sem("vec"))
            elif k == "cache":
                pe.wait_ge(cache_in, 16)
                aux_take(pe, "cache")
                for t in range(KF):
                    turn(bank("cache", 0)[:, 16 * t:16 * (t + 1)], cache[:, P * t:P * (t + 1)],
                         filled_sem("cache") if t == KF - 1 else None)
            elif k == "rstd1":
                pe.wait_ge(acc1_done, 1)
                summed("rstd1", acc)
            elif k == "v":
                h = s[1]
                u, j = (3 if h < HEADS else 7) + h // 2, h % 2
                pe.wait_ge(drained[j], fills(j, u))
                turn_tokens(s, vst[h % 2])
            elif k == "z":
                pe.wait_ge(wg_in, 32)
                pe.wait_ge(drained[1], fills(1, 2))
                aux_take(pe, s)
                for j in range(NJ):
                    small(bank(s, j // 2)[:, 256 * (j % 2):256 * (j % 2 + 1)], ga[0:RANK + 1, P * j:P * (j + 1)],
                          wg[0:RANK + 1, :], done=filled_sem(s) if j == NJ - 1 else None)
            elif k == "zs":
                aux_take(pe, s)
                small(bank(s, 0)[0:NS, 0:256], ga[0:RANK + 1, SEQ:NT], wg[0:RANK + 1, :], done=filled_sem(s))
            elif k == "b":
                p = s[1]
                pe.wait_ge(la_ready, 2)
                pe.wait_ge(c2_in, 16)
                aux_take(pe, s)
                for j in range(NJ):
                    small(bank(s, 0)[:, P * j:P * (j + 1)], la[:, j, P * p:P * (p + 1)], c2[:, C2_U:C2_U + P])
                small(bank(s, 1)[:, 0:NS], las[:, P * p:P * (p + 1)], c2[0:NS, C2_U4:C2_U4 + NS], done=filled_sem(s))
            elif k == "kt":
                pe.wait_ge(qkd_ready, s[1] + 1)
                turn_tokens(s, etl)
            elif k == "gs":
                h = s[1]
                r = slice(GLA_DK * (h % 2), GLA_DK * (h % 2) + GLA_DK)
                pe.wait_ge(qkd_ready, h // 2 + 1)
                aux_take(pe, s)
                for j in range(NJ):
                    c = slice(P * j, P * (j + 1))
                    small(bank(s, 0)[:, c], ebm[r, c], gqk[r, h // 2, c])
                small(bank(s, 1)[0:NS, 0:NS], ebm[r, SEQ:NT], gqk[r, h // 2, SEQ:NT], done=filled_sem(s))
            elif k == "gu":
                p = s[1]
                aux_wait_drained(pe, ("kt", p))
                aux_wait_drained(pe, ("v", 2 * p))
                aux_wait_drained(pe, ("v", 2 * p + 1))
                aux_take(pe, s)
                for h in (2 * p, 2 * p + 1):
                    o = slice(GLA_DK * (h % 2), GLA_DK * (h % 2) + GLA_DK)
                    for c in range(NC):
                        t = slice(CHUNK * (c % 2), CHUNK * (c % 2) + CHUNK)
                        small(bank(s, c % 2)[o, DV * (c // 2):DV * (c // 2 + 1)], ktn[t, c // 2, o],
                              vg[t, c // 2, DV * h:DV * (h + 1)],
                              done=filled_sem(s) if h % 2 and c == NC - 1 else None)
            elif k == "go":
                h = s[1]
                p, r = h // 2, slice(GLA_DK * (h % 2), GLA_DK * (h % 2) + GLA_DK)
                aux_wait_drained(pe, ("gs", h))
                aux_wait_drained(pe, ("gu", p))
                aux_take(pe, s)
                for j in range(NJ):
                    small(bank(s, 0)[:, P * j:P * (j + 1)], vg[:, j, DV * h:DV * (h + 1)], gsc[h % 2][:, j, :], stop=False)
                    for c in (2 * j, 2 * j + 1):
                        if c > 0:
                            t = slice(CHUNK * c, CHUNK * (c + 1))
                            small(bank(s, 0)[:, t], gst[r, p, c - 1, :], gqk[r, p, t], start=False, stop=c % 2 == 1,
                                  done=filled_sem(s) if c == NC - 1 else None)
            elif k == "gx":
                p = s[1]
                aux_wait_drained(pe, ("gs", 2 * p))
                aux_wait_drained(pe, ("gs", 2 * p + 1))
                pe.wait_ge(s0g_in, 16 * (p + 1))
                pe.wait_ge(qbs_ready, 2 * p + 2)
                aux_take(pe, s)
                for i in range(2):
                    h = 2 * p + i
                    small(bank(s, 0)[:, NS * i:NS * (i + 1)], vgs[:, DV * h:DV * (h + 1)], gss[i][:, :], start=i == 0,
                          stop=False)
                out = bank(s, 0)[:, 0:2 * NS].rearrange("p (h t) -> p h t", h=2)
                for b in range(DEC_BATCH):
                    t = slice(DEC_SEQ * b, DEC_SEQ * (b + 1))
                    small(out[:, :, t], s0g[:, b, :], qbs[:, :, t], start=False, stop=b == DEC_BATCH - 1,
                          done=filled_sem(s) if b == DEC_BATCH - 1 else None)
            elif k in ("gw", "rw"):
                h = s[1]
                if k == "gw":
                    pe.wait_ge(gvm_ready, h + 1)
                    pe.wait_ge(k3_ready, h // 2 + 1)
                    vm = gvm
                else:
                    pe.wait_ge(rvm_ready, h + 1)
                    pe.wait_ge(k3_ready, 2 + h + 1)
                    vm = rvm
                aux_take(pe, s)
                for a in range(2):
                    small(bank(s, a), k3[:, :], vm[:, 4 * a:4 * (a + 1), :].rearrange("s b v -> s (b v)"),
                          done=filled_sem(s) if a else None)
            elif k in ("gn", "rn"):
                pe.wait_ge(osq_done, NORMS.index(s) + 1)
                summed(s, gsq)
            elif k == "rk":
                pe.wait_ge(qk_ready, 8)
                turn_tokens(s, qk[:, HEADS + s[1], :])
            elif k == "rs0":
                h = s[1]
                aux_take(pe, s)
                for j in range(2):
                    small(bank(s, j)[:, 0:SEQ - P * j], qk[:, HEADS + h, P * j:P * (j + 1)], qk[:, h, P * j:SEQ],
                          done=filled_sem(s) if j else None)
            elif k == "rs1":
                h = s[1]
                aux_take(pe, s)
                for j in (2, 3):
                    small(bank(s, 0)[:, 2 * P * (j - 2):2 * P * (j - 2) + SEQ - P * j],
                          qk[:, HEADS + h, P * j:P * (j + 1)], qk[:, h, P * j:SEQ])
                small(bank(s, 1)[0:NS, 0:NS], qk[:, HEADS + h, SEQ:NT], qk[:, h, SEQ:NT], done=filled_sem(s))
            elif k == "ro":
                h = s[1]
                aux_wait_drained(pe, ("rs0", h))
                aux_wait_drained(pe, ("rs1", h))
                aux_wait_drained(pe, ("v", HEADS + h))
                pe.wait_ge(s0r_in[h % 2], 16 * (h // 2 + 1))
                aux_take(pe, s)
                for j in range(NJ):
                    small(bank(s, 0)[:, P * j:SEQ], vr[:, j, DV * h:DV * (h + 1)], rsc[:, RS0[j]:RS0[j] + SEQ - P * j],
                          start=j == 0, stop=j == NJ - 1)
                small(bank(s, 1)[:, 0:NS], vrs[:, DV * h:DV * (h + 1)], rss[:, :], stop=False)
                for b in range(DEC_BATCH):
                    t = slice(DEC_SEQ * b, DEC_SEQ * (b + 1))
                    small(bank(s, 1)[:, t], s0r[h % 2][:, b, :], rqs[:, t], start=False, stop=b == DEC_BATCH - 1,
                          done=filled_sem(s) if b == DEC_BATCH - 1 else None)
            elif k == "rp":
                h = s[1]
                aux_wait_drained(pe, ("rk", h))
                aux_take(pe, s)
                for j in range(NJ):
                    small(bank(s, 0)[:, 0:DV], rkn[:, j, :], vr[:, j, DV * h:DV * (h + 1)], start=j == 0,
                          stop=j == NJ - 1, done=filled_sem(s) if j == NJ - 1 else None)

        with pe.Fori(0, 2) as it:
            for n in range(6):
                q, kind = n // 3, n % 3
                u = U_GATE + n
                pe.wait_ge(lo_ready, it * 6 + (u + 1))
                for j in range(2):
                    if kind < 2:
                        pe.wait_ge(drained[j], it * 8 + F0[j] + 4 * q + kind)
                        product(j, u % 2, j, every, nhi, nlo).then_inc(filled[j], 1)
                        continue
                    for b in range(2):
                        pe.wait_ge(drained[b], it * 8 + F0[b] + 4 * q + 2 + j)
                        if n == 2 and j == 0 and b == 0:
                            pe.wait_ge(y_lo, 2 * HEADS)
                        product(b, u % 2, j, every[4 * b:4 * b + 4], yhi, ylo).then_inc(filled[b], 1)
        with pe.Fori(0, 2) as it:
            for n in range(2):
                u = U_WO + n
                pe.wait_ge(lo_ready, it * 2 + (u + 1))
                for j in range(2):
                    pe.wait_ge(drained[j], it * 2 + (FW[j] + n))
                    ready = (lambda kx: pe.wait_ge(m_lo, kx + 1)) if n == 0 and j == 0 else None
                    product(j, u % 2, j, every, mhi, mlo, ready=ready).then_inc(filled[j], 1)

        def up(i, first=False):
            def ready(kx):
                pe.wait_ge(n_lo, KD + kx + 1)
                if kx == KD - 1:
                    pe.wait_ge(acc_done, KD)
                    summed("rstd2", acc)

            for n in range(2):
                u = U_UP + n
                pe.wait_ge(lo_ready, i * 2 + (u + 1))
                for j in range(2):
                    pe.wait_ge(drained[j], i * 2 + (FU[j] + n))
                    product(j, u % 2, j, every, nhi, nlo, ready=ready if first and n == 0 and j == 0 else None
                            ).then_inc(filled[j], 1)

        up(0, first=True)
        with pe.Fori(1, KF // 2) as i:
            up(i)

        def turn_out(*tiles):
            for f in tiles:
                pe.wait_ge(fin_ready, f + 1)
                turn_tokens(("y", f), fin[f % 2])

        for q in range(4):
            for part in range(3):
                u, k0 = U_DOWN + 3 * q + part, 8 * part
                ks = [(k, k0 + k) for k in range(min(8, KF - k0))]
                pe.wait_ge(lo_ready, u + 1)
                if (q, part) == (3, 2):
                    continue
                for j in range(2):
                    if part == 0:
                        pe.wait_ge(drained[j], FD[j] + q)
                    ready = (lambda kx: pe.wait_ge(g_lo, kx + 1)) if q == 0 and j == 0 else None
                    ins = product(j, u % 2, j, ks, ghi, glo, first=part == 0, last=part == 2, ready=ready)
                    if part == 2:
                        ins.then_inc(filled[j], 1)
                    elif j == 1:
                        ins.then_inc(down_part, 1)
                if part == 0 and q > 0:
                    turn_out(2 * q - 2, 2 * q - 1)
                if part == 0 and q == 0:
                    pe.wait_ge(ext_saved, KF)
                    for i in range(3):
                        name = ("tail", i)
                        aux_take(pe, name)
                        for t in range(8 * i, min(8 * i + 8, KF)):
                            m = t - 8 * i
                            turn(bank(name, m // 4)[0:18, P * (m % 4):P * (m % 4 + 1)], pt[:, t, :],
                                 filled_sem(name) if t == min(8 * i + 8, KF) - 1 else None)
        def last_product(e, j):
            product(j, (U_END - 1) % 2, j, [(k, 16 + k) for k in range(KF - 16)], ghi, glo, first=False, banks=(e,)
                    ).then_inc(filled[j], 1)

        def last_sum(e):
            pe.wait_ge(drained[0], FD[0] + 4 + e)
            pe.wait_ge(last_acc, e + 1)
            for n, sq in enumerate((facc, osq[1])):
                if n == 1:
                    pe.wait_ge(last_sq, 2 * e + 2)
                for j in (2 * e, 2 * e + 1):
                    done = last_sums if e == 0 and n == 1 and j == 1 else None
                    small(mm[:, e, j:j + 1], sq[:, P * j:P * (j + 1)], ones[:, 0:1], start=n == 0 and j == 2 * e,
                          stop=n == 1, done=done)
                if e == 1:
                    small(mm[0:NS, e, NJ:NJ + 1], sq[:, SEQ:NT], ones[:, 0:1], start=False, stop=n == 1,
                          done=last_sums if n == 1 else None)

        def last_turn(e):
            name = ("ye", e)
            pe.wait_ge(last_fin, 2 * e + 2)
            aux_take(pe, name)
            for f in range(2):
                for t in range(2):
                    turn(bank(name, 0)[:, P * (2 * f + t):P * (2 * f + t + 1)], fin[f][:, P * (2 * e + t):P * (2 * e + t + 1)],
                         filled_sem(name) if e == 0 and (f, t) == (1, 1) else None)
            if e == 1:
                for f in range(2):
                    turn(bank(name, 1)[0:NS, P * f:P * (f + 1)], fin[f][:, SEQ:NT], filled_sem(name) if f else None)

        last_product(0, 0)
        last_product(0, 1)
        last_product(1, 0)
        last_sum(0)
        last_turn(0)
        last_product(1, 1)
        last_sum(1)
        last_turn(1)

    ctx.close()


INPUTS = ["x_prompt", "x_sample", "state_ret", "state_gla", "cache_conv", "ln1", "w_in", "w_gate_up", "b_gate_up",
          "g_ret", "g_gla", "w_ret_out", "w_gla_out", "w_o", "ln2", "w_up", "conv_w", "conv_b", "w_down", "ln_f"]
OUTPUTS = [(1, SEQ, D_MODEL), (DEC_BATCH, DEC_SEQ, D_MODEL), (1, 1, HEADS, RET_DK, DV), (1, DEC_BATCH, HEADS, RET_DK, DV),
           (1, 1, HEADS, GLA_DK, DV), (1, DEC_BATCH, HEADS, GLA_DK, DV), (1, 1, CONV_WIDTH - 1, D_FF),
           (1, DEC_BATCH, CONV_WIDTH - 1, D_FF)]


def kernel(**inputs):
    import concourse.bacc as bacc
    from concourse.bass_utils import run_bass_kernel_spmd

    nc = bacc.Bacc("TRN2", target_bir_lowering=False, num_devices=1)
    arrays, aps = {}, {}
    for name, a in [(n, inputs[n]) for n in INPUTS] + list(zip(("c1", "c2", "decay", "rope"), constants())):
        a = np.ascontiguousarray(a)
        arrays[f"in_{name}"] = a
        aps[name] = nc.dram_tensor(f"in_{name}", a.shape, mybir.dt.from_np(a.dtype), kind="ExternalInput").ap()
    outs = [nc.dram_tensor(f"out_{i}", shape, F32, kind="ExternalOutput").ap() for i, shape in enumerate(OUTPUTS)]
    build(nc, aps, outs)
    r = run_bass_kernel_spmd(nc, [arrays], core_ids=[0])
    return tuple(r.results[0][f"out_{i}"] for i in range(len(OUTPUTS)))
```
